# Optimizing a Trainium2 kernel written in Bass

```python
import math
import jax, jax.numpy as jnp
from jax import lax
import numpy as np

D_MODEL = 1024
BATCH = 1
SEQ = 256
DEPTH = 2

N_MIXERS = 2
DIFF_HEAD_DIM = 64
DIFF_HEADS = D_MODEL // (2 * DIFF_HEAD_DIM)
MOBA_HEAD_DIM = 64
MOBA_HEADS = D_MODEL // MOBA_HEAD_DIM
MOBA_BLOCK = 256
MOBA_TOPK = 3
Q_BLOCK = 128
MOBA_Q_CHUNK = 16
D_FF = 2816
N_EXPERTS = 8
TOP_K_EXPERTS = 2
D_EXPERT = 3584
NORM_EPS = 1e-6
SUBLN_EPS = 1e-5
N_DIFF_LAYERS = (DEPTH + 1) // 2
N_MOBA_LAYERS = DEPTH // 2

kernel_name = 'hybrid_diffattn_moba_moe_trunk'

def alibi_slopes(n_heads):
    return jnp.asarray(2.0 ** (-8.0 * np.arange(1, n_heads + 1) / n_heads), dtype=jnp.float32)

def rms_norm(x, g, eps=NORM_EPS):
    x32 = x.astype(jnp.float32)
    y = x32 * lax.rsqrt(jnp.mean(x32 * x32, axis=-1, keepdims=True) + eps)
    return (y * g.astype(jnp.float32)).astype(x.dtype)

def swiglu(u, w_gate, w_up, w_down):
    return (jax.nn.silu(u @ w_gate) * (u @ w_up)) @ w_down

def diff_attention(h, w_qkv, w_o, lam, subln, layer_idx):
    B, S, _ = h.shape
    H, d = DIFF_HEADS, DIFF_HEAD_DIM
    q, k, v = jnp.split(h @ w_qkv, 3, axis=-1)
    q = q.reshape(B, S, H, 2, d).transpose(0, 2, 3, 1, 4)
    k = k.reshape(B, S, H, 2, d).transpose(0, 2, 3, 1, 4)
    v = v.reshape(B, S, H, 2 * d).transpose(0, 2, 1, 3)
    lam_init = 0.8 - 0.6 * math.exp(-0.3 * layer_idx)
    l32 = lam.astype(jnp.float32)
    lam_full = jnp.exp(jnp.sum(l32[0] * l32[1])) - jnp.exp(jnp.sum(l32[2] * l32[3])) + lam_init
    slopes = alibi_slopes(H)
    key_pos = jnp.arange(S)
    scale = d ** -0.5

    def query_block(start):
        qb = lax.dynamic_slice_in_dim(q, start, Q_BLOCK, axis=3)
        s = jnp.einsum('bhiqd,bhikd->bhiqk', qb, k).astype(jnp.float32) * scale
        dist = (start + jnp.arange(Q_BLOCK))[:, None] - key_pos[None, :]
        bias = -slopes[:, None, None] * dist.astype(jnp.float32)
        s = jnp.where(dist >= 0, s + bias[None, :, None], -jnp.inf)
        p = jax.nn.softmax(s, axis=-1)
        a = p[:, :, 0] - lam_full * p[:, :, 1]
        return jnp.einsum('bhqk,bhkd->bhqd', a.astype(v.dtype), v)

    o = lax.map(query_block, jnp.arange(0, S, Q_BLOCK))
    o = o.transpose(1, 0, 3, 2, 4).reshape(B, S, H, 2 * d)
    o = rms_norm(o, subln, SUBLN_EPS) * (1.0 - lam_init)
    return o.reshape(B, S, H * 2 * d) @ w_o

def moba_attention(h, w_qkv, w_o):
    B, S, _ = h.shape
    H, d, BLK = MOBA_HEADS, MOBA_HEAD_DIM, MOBA_BLOCK
    q, k, v = jnp.split(h @ w_qkv, 3, axis=-1)
    q = q.reshape(B, S, H, d).transpose(0, 2, 1, 3)
    k = k.reshape(B, S, H, d).transpose(0, 2, 1, 3)
    v = v.reshape(B, S, H, d).transpose(0, 2, 1, 3)
    NB = -(-S // BLK)
    pad = NB * BLK - S
    k_blocks = jnp.pad(k, ((0, 0), (0, 0), (0, pad), (0, 0))).reshape(B, H, NB, BLK, d)
    v_blocks = jnp.pad(v, ((0, 0), (0, 0), (0, pad), (0, 0))).reshape(B, H, NB, BLK, d)
    k_mean = jnp.mean(k_blocks, axis=3)
    k_eff = min(MOBA_TOPK, NB)
    b_idx = jnp.arange(B)[:, None, None, None]
    h_idx = jnp.arange(H)[None, :, None, None]
    slopes = alibi_slopes(H)
    scale = d ** -0.5

    def query_chunk(start):
        qc = lax.dynamic_slice_in_dim(q, start, MOBA_Q_CHUNK, axis=2)
        t = start + jnp.arange(MOBA_Q_CHUNK)
        own = start // BLK
        gate = jnp.einsum('bhqd,bhnd->bhqn', qc, k_mean).astype(jnp.float32)
        gate = jnp.where(jnp.arange(NB) < own, gate, -jnp.inf)
        _, sel = lax.top_k(gate, k_eff)
        valid = jnp.arange(k_eff) < own
        k_sel = k_blocks[b_idx, h_idx, sel]
        v_sel = v_blocks[b_idx, h_idx, sel]
        s_sel = jnp.einsum('bhqd,bhqjsd->bhqjs', qc, k_sel).astype(jnp.float32) * scale
        pos_sel = sel[..., None] * BLK + jnp.arange(BLK)
        dist_sel = (t[:, None, None] - pos_sel).astype(jnp.float32)
        s_sel = jnp.where(valid[:, None], s_sel - slopes[None, :, None, None, None] * dist_sel, -jnp.inf)
        k_own = lax.dynamic_index_in_dim(k_blocks, own, axis=2, keepdims=False)
        v_own = lax.dynamic_index_in_dim(v_blocks, own, axis=2, keepdims=False)
        s_own = jnp.einsum('bhqd,bhsd->bhqs', qc, k_own).astype(jnp.float32) * scale
        dist_own = t[:, None] - (own * BLK + jnp.arange(BLK))[None, :]
        s_own = jnp.where(dist_own >= 0,
                          s_own - slopes[None, :, None, None] * dist_own.astype(jnp.float32),
                          -jnp.inf)
        scores = jnp.concatenate([s_sel.reshape(B, H, MOBA_Q_CHUNK, k_eff * BLK), s_own], axis=-1)
        p = jax.nn.softmax(scores, axis=-1).astype(v.dtype)
        p_sel = p[..., :k_eff * BLK].reshape(B, H, MOBA_Q_CHUNK, k_eff, BLK)
        p_own = p[..., k_eff * BLK:]
        return (jnp.einsum('bhqjs,bhqjsd->bhqd', p_sel, v_sel)
                + jnp.einsum('bhqs,bhsd->bhqd', p_own, v_own))

    o = lax.map(query_chunk, jnp.arange(0, S, MOBA_Q_CHUNK))
    o = o.transpose(1, 0, 3, 2, 4).reshape(B, S, H * d)
    return o @ w_o

def moe_swiglu(h, router, w_gate, w_up, w_down):
    B, S, D = h.shape
    tok = h.reshape(B * S, D)
    logits = (tok @ router).astype(jnp.float32)
    top_v, top_i = lax.top_k(logits, TOP_K_EXPERTS)
    w = jax.nn.softmax(top_v, axis=-1)
    gates = jnp.sum(jax.nn.one_hot(top_i, N_EXPERTS, dtype=jnp.float32) * w[..., None], axis=1)
    out = jnp.zeros_like(tok)
    for e in range(N_EXPERTS):
        out = out + gates[:, e:e + 1].astype(tok.dtype) * swiglu(tok, w_gate[e], w_up[e], w_down[e])
    return out.reshape(B, S, D)

def setup_inputs(seed: int = 0) -> dict:
    key = jax.random.key(seed)
    ks = jax.random.split(key, 18)
    D = D_MODEL
    nrm = jax.random.normal
    return {
        'x': nrm(ks[0], (BATCH, SEQ, D), jnp.float32),
        'norm_mix': 1.0 + 0.02 * nrm(ks[1], (DEPTH, D), jnp.float32),
        'norm_ffn': 1.0 + 0.02 * nrm(ks[2], (DEPTH, D), jnp.float32),
        'diff_w_qkv': nrm(ks[3], (N_DIFF_LAYERS, D, 3 * D), jnp.float32) * D ** -0.5,
        'diff_w_o': nrm(ks[4], (N_DIFF_LAYERS, D, D), jnp.float32) * D ** -0.5,
        'diff_lambda': 0.1 * nrm(ks[5], (N_DIFF_LAYERS, 4, DIFF_HEAD_DIM), jnp.float32),
        'diff_subln': 1.0 + 0.02 * nrm(ks[6], (N_DIFF_LAYERS, 2 * DIFF_HEAD_DIM), jnp.float32),
        'moba_w_qkv': nrm(ks[7], (N_MOBA_LAYERS, D, 3 * D), jnp.float32) * D ** -0.5,
        'moba_w_o': nrm(ks[8], (N_MOBA_LAYERS, D, D), jnp.float32) * D ** -0.5,
        'ffn_w_gate': nrm(ks[9], (N_DIFF_LAYERS, D, D_FF), jnp.float32) * D ** -0.5,
        'ffn_w_up': nrm(ks[10], (N_DIFF_LAYERS, D, D_FF), jnp.float32) * D ** -0.5,
        'ffn_w_down': nrm(ks[11], (N_DIFF_LAYERS, D_FF, D), jnp.float32) * D_FF ** -0.5,
        'moe_router': nrm(ks[12], (N_MOBA_LAYERS, D, N_EXPERTS), jnp.float32) * D ** -0.5,
        'moe_w_gate': nrm(ks[13], (N_MOBA_LAYERS, N_EXPERTS, D, D_EXPERT), jnp.float32) * D ** -0.5,
        'moe_w_up': nrm(ks[14], (N_MOBA_LAYERS, N_EXPERTS, D, D_EXPERT), jnp.float32) * D ** -0.5,
        'moe_w_down': nrm(ks[15], (N_MOBA_LAYERS, N_EXPERTS, D_EXPERT, D), jnp.float32) * D_EXPERT ** -0.5,
        'final_norm': 1.0 + 0.02 * nrm(ks[16], (D,), jnp.float32),
    }

def reference(x, norm_mix, norm_ffn, diff_w_qkv, diff_w_o, diff_lambda, diff_subln,
              moba_w_qkv, moba_w_o, ffn_w_gate, ffn_w_up, ffn_w_down,
              moe_router, moe_w_gate, moe_w_up, moe_w_down, final_norm):
    h = x
    for i in range(DEPTH):
        j = i // N_MIXERS
        u = rms_norm(h, norm_mix[i])
        if i % N_MIXERS == 0:
            mix = diff_attention(u, diff_w_qkv[j], diff_w_o[j], diff_lambda[j], diff_subln[j], i)
        else:
            mix = moba_attention(u, moba_w_qkv[j], moba_w_o[j])
        h = h + mix
        u = rms_norm(h, norm_ffn[i])
        if i % 2 == 0:
            ffn = swiglu(u, ffn_w_gate[j], ffn_w_up[j], ffn_w_down[j])
        else:
            ffn = moe_swiglu(u, moe_router[j], moe_w_gate[j], moe_w_up[j], moe_w_down[j])
        h = h + ffn
    return rms_norm(h, final_norm)


_drawn_inputs = setup_inputs


def setup_inputs(seed=0):
    import zlib

    import numpy as np

    out = dict(_drawn_inputs(seed))
    spreads = {}
    factors = {}
    for name, (base, spread) in spreads.items():
        noise = np.random.default_rng([zlib.crc32(name.encode()), seed]).standard_normal(out[name].shape)
        drawn = base * np.exp(spread * noise) if base else spread * noise
        out[name] = __import__('jax').numpy.asarray(drawn.astype(out[name].dtype))
    for name, factor in factors.items():
        out[name] = (out[name] * factor).astype(out[name].dtype)
    return out
```

```python
import math
from contextlib import ExitStack

import numpy as np
import concourse.bass as bass
from concourse import mybir

F32 = mybir.dt.float32
F32R = mybir.dt.float32r
I32 = mybir.dt.int32
U32 = mybir.dt.uint32
ALU = mybir.AluOpType
ACT = mybir.ActivationFunctionType
AX = mybir.AxisListType

P = 128
GROUP = 512
RING = 7
HL = 6
AHEAD = 5
GS = 8
SLOT = GS * GROUP
POOL_EVERY = 4
POOL_GS = GS // POOL_EVERY
BIG = 1e30


def trunk(nc, x, norm_mix, norm_ffn, diff_w_qkv, diff_w_o, diff_lambda, diff_subln, moba_w_qkv, moba_w_o,
          ffn_w_gate, ffn_w_up, ffn_w_down, moe_router, moe_w_gate, moe_w_up, moe_w_down, final_norm, out):
    _, T, D = x.shape
    TB = T // P
    KD = D // P
    FF = ffn_w_gate.shape[2]
    E, DE = moe_w_gate.shape[1], moe_w_gate.shape[3]
    W = 512
    NF = -(-FF // W)
    NE = DE // W
    FBW = W // P
    PAIRS = D // P
    UNITS = PAIRS * TB
    EPS, SUB_EPS, SUB = 1e-6, 1e-5, 1.0 - (0.8 - 0.6 * math.exp(0.0))
    LAM_INIT = 0.8 - 0.6 * math.exp(0.0)
    SCALE = 64 ** -0.5
    assert T == 2 * P and D == 1024 and DE % W == 0 and 2 * T // (P + 1) <= 3
    slopes = [[2.0 ** (-8.0 * (p + 1) / PAIRS) for p in range(PAIRS) for _ in range(2)],
              [2.0 ** (-8.0 * (h + 1) / (2 * PAIRS)) for h in range(2 * PAIRS)]]

    slots = []

    def cols(w, k, c, n):
        return w[0].rearrange("(k p) n -> p k n", p=P)[:, :, c:c + n]

    def rows(w, r, n):
        return w[0][r:r + n, :].rearrange("(g p) n -> p g n", p=P)

    first_slot = {}
    for layer, (wqkv, wo) in enumerate(((diff_w_qkv, diff_w_o), (moba_w_qkv, moba_w_o))):
        first_slot["qkv", layer] = len(slots)
        for c in (0, D, W, D + W, 2 * D, 2 * D + W):
            slots.append((cols(wqkv, KD, c, W), GS))
        first_slot["wo", layer] = len(slots)
        for r in (0, W):
            slots.append((rows(wo, r, W), GS))
        if layer == 0:
            first_slot["ffn", 0] = len(slots)
            width = [min(W, FF - c * W) for c in range(NF)]
            gate_slot, up_slot, down_slot = {}, {}, {}
            for c in range(NF + 1):
                if c < NF:
                    gate_slot[c] = len(slots)
                    slots.append((cols(ffn_w_gate, KD, c * W, width[c]), width[c] * KD // GROUP))
                    up_slot[c] = len(slots)
                    slots.append((cols(ffn_w_up, KD, c * W, width[c]), width[c] * KD // GROUP))
                if c > 0:
                    down_slot[c - 1] = len(slots)
                    slots.append((rows(ffn_w_down, (c - 1) * W, width[c - 1]), width[c - 1] // P * D // GROUP))
    NS = len(slots)
    first_group = [sum(g for _, g in slots[:s]) for s in range(NS + 1)]
    NG = first_group[NS]
    group_of = [(s, g) for s in range(NS) for g in range(slots[s][1])]
    by_pool = [g % POOL_EVERY == POOL_EVERY - 1 for _, g in group_of]
    pool_upto = [sum(by_pool[:n]) for n in range(NG + 1)]
    dve_upto = [n - pool_upto[n] for n in range(NG + 1)]

    item_slots = [("gate", 0), ("up", 0)]
    for c in range(1, NE):
        item_slots += [("gate", c), ("up", c), ("down", c - 1)]
    item_slots += [("down", NE - 1)]
    item_slot = {key: j for j, key in enumerate(item_slots)}
    IS = len(item_slots)
    IG = GS * IS
    assert IS % RING == 0 and IG % HL == 0 and all(g == GS for _, g in slots[-RING:])

    with ExitStack() as ctx:
        def sb(name, shape, dt=F32, stack=ctx):
            return stack.enter_context(nc.sbuf_tensor(name, shape, dt))

        def sem(name):
            return ctx.enter_context(nc.semaphore(name))

        ring = sb("ring", [P, RING, SLOT])
        whi = sb("whi", [P, HL, GROUP], F32R)
        wlo = sb("wlo", [P, HL, GROUP], F32R)
        xhi = sb("xhi", [P, KD, T], F32R)
        xlo = sb("xlo", [P, KD, T], F32R)
        res = sb("res", [P, TB, D])
        rowbuf = sb("rowbuf", [P, TB, D])
        rt = sb("rt", [P, KD, E])
        expert_no = sb("expert_no", [P, E])
        ident = sb("ident", [P, P])
        ones = sb("ones", [P, P])
        before = sb("before", [P, P])
        slotno = sb("slotno", [P, P])
        gain_rows = sb("gain_rows", [40, P])
        gain_cols = sb("gain_cols", [P, 40])
        small = sb("small", [P, 16])
        ssq = sb("ssq", [P, 5, TB])
        rstd = sb("rstd", [P, 5, TB])
        q_scale = sb("q_scale", [P, 2, PAIRS])
        halfneg = sb("halfneg", [P, 2 * PAIRS])
        score_min = sb("score_min", [P, 2, UNITS, 2])
        prob_sum = sb("prob_sum", [P, 2, UNITS, 2])
        prob_inv = sb("prob_inv", [P, 2, UNITS, 2])
        mix = sb("mix", [P, UNITS])
        head_ssq = sb("head_ssq", [P, TB, PAIRS])
        head_rstd = sb("head_rstd", [P, TB, PAIRS])

        attn = ExitStack()
        qT = sb("qT", [P, PAIRS, T], F32, attn)
        kT = sb("kT", [P, PAIRS, T], F32, attn)
        val = sb("val", [P, TB, D], F32, attn)
        probs = sb("probs", [P, 2, 2, T], F32, attn)
        lam = probs[:, 0, 0, :].rearrange("p (a d) -> p a d", a=4)
        lam_prod = probs[:, 0, 1, 0:64]
        junk = sb("junk", [P, P], F32, attn)
        probsT = sb("probsT", [P, 2, 4, P], F32, attn)
        dist = sb("dist", [P, 3 * P], F32, attn)
        attn.close()
        hid = sb("hid", [P, TB, W])
        gain = hid[:, :, :].rearrange("p b n -> p (b n)")
        hhi = sb("hhi", [P, FBW, T], F32R)
        hlo = sb("hlo", [P, FBW, T], F32R)
        ihi = sb("ihi", [P, KD, P], F32R)
        ilo = sb("ilo", [P, KD, P], F32R)
        yhi = sb("yhi", [P, D], F32R)
        ylo = sb("ylo", [P, D], F32R)
        pick = sb("pick", [P, TB, P], F32R)
        pickT = sb("pickT", [P, T], F32R)
        eqA = sb("eqA", [P, TB, P])
        eqB = sb("eqB", [P, TB, P])
        gate_of_slot = sb("gate_of_slot", [P, 1])
        rt_hi = sb("rt_hi", [P, KD, E], F32R)
        rt_lo = sb("rt_lo", [P, KD, E], F32R)
        logit = sb("logit", [P, TB, E])
        top = sb("top", [P, TB, E])
        top_at = sb("top_at", [P, TB, E], U32)
        top_atf = sb("top_atf", [P, TB, E])
        isA = sb("isA", [P, TB, E])
        isB = sb("isB", [P, TB, E])
        member = sb("member", [P, TB, E])
        pos = sb("pos", [P, 3, E])
        over = sb("over", [P, E])
        over_before = sb("over_before", [P, E])
        far = sb("far", [P, TB, E])
        jump = sb("jump", [P, E])
        place = sb("place", [P, TB, E])
        tmpE = sb("tmpE", [P, TB, E])
        key = sb("key", [P, 2, TB])
        wgt = sb("wgt", [P, 2, TB])
        wtmp = sb("wtmp", [P, 2, TB])
        extra_f = sb("extra_f", [P, 4])
        extra = sb("extra", [P, 4], I32)

        psA = ctx.enter_context(nc.psum_tensor("psA", [P, 2, W], F32))
        psB = ctx.enter_context(nc.psum_tensor("psB", [P, 2, W], F32))
        psY = ctx.enter_context(nc.psum_tensor("psY", [P, 4, W], F32))

        x_in = sem("x_in")
        small_in = sem("small_in")
        gain_in = sem("gain_in")
        router_in = sem("router_in")
        slot_full = [sem(f"slot_full{r}") for r in range(RING)]
        hi_done = sem("hi_done")
        lo_dve = sem("lo_dve")
        lo_pool = sem("lo_pool")
        group_used = sem("group_used")
        consts = sem("consts")
        ones_set = sem("ones_set")
        gains_T = sem("gains_T")
        gains_set = sem("gains_set")
        lam_exp = sem("lam_exp")
        lam_dot = sem("lam_dot")
        ssq_done = sem("ssq_done")
        rstd_done = sem("rstd_done")
        rows_done = sem("rows_done")
        turn_done = sem("turn_done")
        xhi_done = sem("xhi_done")
        xlo_done = sem("xlo_done")
        qkv_done = sem("qkv_done")
        score_done = sem("score_done")
        min_done = sem("min_done")
        exp_done = sem("exp_done")
        mixed = sem("mixed")
        probT_done = sem("probT_done")
        probT_out = sem("probT_out")
        pv_done = sem("pv_done")
        o_done = sem("o_done")
        o_ssq = sem("o_ssq")
        o_rstd = sem("o_rstd")
        res_done = sem("res_done")
        silu_done = sem("silu_done")
        hid_done = sem("hid_done")
        hidT_done = sem("hidT_done")
        hhi_done = sem("hhi_done")
        hlo_done = sem("hlo_done")
        chain_dve = sem("chain_dve")
        chain_pool = sem("chain_pool")
        chain_act = sem("chain_act")
        rt_split = sem("rt_split")
        logit_mm = sem("logit_mm")
        rowsplit = sem("rowsplit")
        wdiff = sem("wdiff")
        wexp = sem("wexp")
        member_set = sem("member_set")
        pos_mm = sem("pos_mm")
        table_set = sem("table_set")
        pick_set = sem("pick_set")
        gather_mm = sem("gather_mm")
        ihi_done = sem("ihi_done")
        ilo_done = sem("ilo_done")
        pickT_mm = sem("pickT_mm")
        pickT_set = sem("pickT_set")
        yhi_done = sem("yhi_done")
        ylo_done = sem("ylo_done")
        scatter_mm = sem("scatter_mm")
        add_done = sem("add_done")
        m_silu = sem("m_silu")
        m_hid = sem("m_hid")
        m_hidT = sem("m_hidT")
        m_hhi = sem("m_hhi")
        m_hlo = sem("m_hlo")
        out_rows = sem("out_rows")
        stored = sem("stored")

        block = ctx.enter_context(nc.Block())

        def f(ap):
            return ap.bitcast(F32)

        def ring_group(s, g):
            return ring[:, s % RING, g * GROUP:(g + 1) * GROUP]

        def wait_group(eng, n):
            if by_pool[n]:
                eng.wait_ge(lo_pool, pool_upto[n + 1])
            else:
                eng.wait_ge(lo_dve, dve_upto[n + 1])

        def n_items(eng):
            eng.wait_ge(table_set, 1)
            return eng.value_load(extra[0:1, 0:1], min_val=0, max_val=3) + E

        def slot_landed(i, j):
            r = (NS + j) % RING
            dense = sum(1 for s in range(NS) if s % RING == r)
            return i * (16 * IS // RING) + 16 * (dense + j // RING + 1)

        def used_at(i, m):
            return i * IG + (NG + m)

        def wait_item_group(eng, i, m):
            pool_m, rest = divmod(m, POOL_EVERY)
            if rest == POOL_EVERY - 1:
                eng.wait_ge(lo_pool, i * (IG // POOL_EVERY) + (pool_upto[NG] + pool_m + 1))
            else:
                eng.wait_ge(lo_dve, i * (IG - IG // POOL_EVERY) + (dve_upto[NG] + m - pool_m + 1))

        BUILDS = [("norm", 0), ("attn", 0), ("norm", 1), ("norm", 2), ("attn", 1), ("norm", 3)]
        ROWS_BEFORE = [0, 2, 4, 6, None, 8]
        ROWS_GAINED = 11

        @block.sync
        def _(sp):
            sp.dma_start(res[:, :, :], x[0].rearrange("(b p) d -> p b d", p=P)).then_inc(x_in, 16)

            for s, (src, groups) in enumerate(slots):
                if s >= RING:
                    n = first_group[s - RING + 1]
                    sp.wait_ge(lo_dve, dve_upto[n])
                    sp.wait_ge(lo_pool, pool_upto[n])
                dst = ring[:, s % RING, 0:groups * GROUP].rearrange("p (k n) -> p k n", n=src.shape[2])
                sp.dma_start(dst, src).then_inc(slot_full[s % RING], 16)

            dve_past = sp.alloc_register("dve_past")
            pool_past = sp.alloc_register("pool_past")
            sp.reg_mov(dve_past, dve_upto[NG] + (GS - POOL_GS) * (1 - RING))
            sp.reg_mov(pool_past, pool_upto[NG] + POOL_GS * (1 - RING))

            def load(r, dst, src):
                sp.wait_ge(lo_dve, dve_past)
                sp.wait_ge(lo_pool, pool_past)
                sp.dma_start(dst, src).then_inc(slot_full[r], 16)
                sp.reg_add(dve_past, dve_past, GS - POOL_GS)
                sp.reg_add(pool_past, pool_past, POOL_GS)

            def item(e):
                for j, (kind, c) in enumerate(item_slots):
                    r = (NS + j) % RING
                    if kind == "down":
                        src = moe_w_down[0][e, c * W:(c + 1) * W, :].rearrange("(g p) n -> p g n", p=P)
                    else:
                        w = moe_w_gate if kind == "gate" else moe_w_up
                        src = w[0][e, :, c * W:(c + 1) * W].rearrange("(k p) n -> p k n", p=P)
                    load(r, ring[:, r, :].rearrange("p (k n) -> p k n", n=src.shape[2]), src)

            with sp.Fori(0, E) as i:
                item(i)
            n = n_items(sp)
            with sp.If(n > E):
                with sp.Fori(E, n) as i:
                    e = sp.value_load(extra[0:1, bass.ds(i - (E - 1), 1)], min_val=0, max_val=E - 1)
                    item(e)
            r = NS % RING
            load(r, ring[:, r, 0:2], moe_w_down[0][0, 0:P, 0:2])
            for tb in range(TB):
                sp.wait_ge(out_rows, tb + 1)
                sp.dma_start(out[0, tb * P:(tb + 1) * P, :], rowbuf[:, tb, :]).then_inc(stored, 16)
            sp.wait_ge(stored, 16 * TB)

        @block.scalar
        def _(act):
            for row, src in ((0, norm_mix[0]), (KD, norm_ffn[0]), (2 * KD, norm_mix[1]), (3 * KD, norm_ffn[1])):
                act.dma_start(gain_rows[row:row + KD, :], src.rearrange("(k p) -> k p", p=P)).then_inc(small_in, 16)
            act.dma_start(gain_rows[4 * KD:4 * KD + 1, :], diff_subln[:, :]).then_inc(small_in, 16)
            act.dma_start(lam, diff_lambda[0].partition_broadcast(P)).then_inc(small_in, 16)
            act.dma_start(rt[:, :, :], moe_router[0].rearrange("(k p) e -> p k e", p=P)).then_inc(router_in, 16)

            split = [0]

            def split_to(n):
                for m in range(split[0], min(n, NG)):
                    s, g = group_of[m]
                    if g == 0:
                        act.wait_ge(slot_full[s % RING], 16 * (s // RING + 1))
                    if m >= HL:
                        act.wait_ge(group_used, m - HL + 1)
                    nc.scalar.copy(whi[:, m % HL, :], ring_group(s, g)).then_inc(hi_done, 1)
                split[0] = max(split[0], min(n, NG))

            def square_sums(norm, arrived):
                for tb in range(TB):
                    act.wait_ge(*arrived(tb))
                    nc.scalar.activation(rowbuf[:, tb, :], res[:, tb, :], ACT.Square,
                                         accum_out=ssq[:, norm, tb:tb + 1]).then_inc(ssq_done, 1)

            def build(b):
                kind, j = BUILDS[b]
                for q in range(KD // 2):
                    act.wait_ge(turn_done, 4 * b + q + 1)
                    if kind == "norm":
                        for k in range(2 * q, 2 * q + 2):
                            col = (0, KD, 2 * KD, 3 * KD)[j] + k
                            ins = nc.scalar.activation(xhi[:, k, :], psY[:, q, (k % 2) * T:(k % 2 + 1) * T], ACT.Copy,
                                                       scale=gain_cols[:, col:col + 1])
                    elif j == 0:
                        ins = nc.scalar.activation(xhi[:, 2 * q:2 * q + 2, :], psY[:, q, :], ACT.Copy,
                                                   scale=gain_cols[:, 4 * KD:4 * KD + 1])
                    else:
                        ins = nc.scalar.copy(xhi[:, 2 * q:2 * q + 2, :], psY[:, q, :])
                    ins.then_inc(xhi_done, 1)

            def exps(layer, u):
                n = UNITS * layer + u
                keys = (u % TB + 1) * P
                if u >= 2:
                    act.wait_ge(probT_done, n - 1)
                act.wait_ge(min_done, n + 1)
                for i in range(2):
                    ins = nc.scalar.activation(probs[:, u % 2, i, 0:keys], psY[:, 2 * (u % 2) + i, 0:keys], ACT.Exp,
                                               scale=-1.0, bias=score_min[:, layer, u, i:i + 1],
                                               accum_out=prob_sum[:, layer, u, i:i + 1])
                ins.then_inc(exp_done, 1)

            def copy_probT(u):
                blocks = u % TB + 1
                act.wait_ge(probT_done, u + 1)
                if u >= 2:
                    act.wait_ge(pv_done, u - 1)
                nc.scalar.copy(probsT[:, u % 2, 0:blocks, :], psA[:, u % 2, 0:blocks * P]).then_inc(probT_out, 1)

            split_to(HL)
            square_sums(0, lambda tb: (x_in, 16))
            act.wait_ge(lam_dot, 1)
            nc.scalar.activation(small[:, 2:4], small[:, 0:2], ACT.Exp).then_inc(lam_exp, 1)
            act.wait_ge(gains_set, 1)
            for layer in range(2):
                if layer == 1:
                    square_sums(2, lambda tb: (res_done, TB + tb + 1))
                build(3 * layer)
                s0 = first_slot["qkv", layer]
                for j in range(6):
                    split_to(first_group[s0 + j + 1] + AHEAD)
                    act.wait_ge(group_used, first_group[s0 + j + 1])
                    ps = psA if j % 2 == 0 else psB
                    if j in (0, 2):
                        for b in range(4):
                            pair = 2 * j + b
                            ins = nc.scalar.activation(qT[:, pair, :], ps[:, b // 2, (b % 2) * T:(b % 2 + 1) * T],
                                                       ACT.Copy, scale=q_scale[:, layer, pair:pair + 1])
                    elif j in (1, 3):
                        ins = nc.scalar.copy(kT[:, 2 * j - 2:2 * j + 2, :], ps[:, :, :])
                    else:
                        ins = nc.scalar.copy(val[:, :, (j - 4) * W:(j - 3) * W], ps[:, :, :])
                    ins.then_inc(qkv_done, 1)
                split_to(first_group[first_slot["wo", layer]] + HL)
                for u in range(UNITS):
                    exps(layer, u)
                    if layer == 0 and u >= 1:
                        copy_probT(u - 1)
                if layer == 0:
                    copy_probT(UNITS - 1)
                build(3 * layer + 1)
                if layer == 1:
                    act.dma_start(gain, norm_ffn[1].partition_broadcast(P)).then_inc(gain_in, 16)
                split_to(first_group[first_slot["wo", layer] + 2] + HL)
                square_sums(2 * layer + 1, lambda tb: (res_done, 2 * TB * layer + tb + 1))
                if layer == 0:
                    build(2)
                    for c in range(NF):
                        w = width[c]
                        split_to(first_group[gate_slot[c] + 1] + AHEAD)
                        act.wait_ge(group_used, first_group[gate_slot[c] + 1])
                        nc.scalar.activation(hid[:, :, 0:w], psA[:, :, 0:w], ACT.Silu).then_inc(silu_done, 1)
                        last = down_slot[c - 1] if c else up_slot[c]
                        split_to(first_group[last + 1] + AHEAD)
                        for q in range(w // (2 * P)):
                            act.wait_ge(hidT_done, 2 * c + q + 1)
                            nc.scalar.copy(hhi[:, 2 * q:2 * q + 2, :], psB[:, q, :]).then_inc(hhi_done, 1)
                    split_to(first_group[first_slot["qkv", 1]] + HL)

            act.wait_ge(router_in, 16)
            nc.scalar.copy(rt_hi[:, :, :], rt[:, :, :]).then_inc(rt_split, 1)
            build(5)
            act.wait_ge(wdiff, 1)
            nc.scalar.activation(wtmp[:, 0, :], wtmp[:, 1, :], ACT.Exp).then_inc(wexp, 1)
            act.wait_ge(rows_done, ROWS_GAINED)
            act.wait_ge(logit_mm, 1)
            nc.scalar.copy(xhi[:, :, :].rearrange("p k t -> p (k t)"),
                           rowbuf[:, :, :].rearrange("p b d -> p (b d)")).then_inc(rowsplit, 1)

            def item_split(i, first, last):
                for m in range(first, last):
                    j, g = m // GS, m % GS
                    r = (NS + j) % RING
                    if g == 0:
                        act.wait_ge(slot_full[r], slot_landed(i, j))
                    act.wait_ge(group_used, used_at(i, m - HL + 1))
                    nc.scalar.copy(whi[:, (NG + m) % HL, :], ring[:, r, g * GROUP:(g + 1) * GROUP]).then_inc(hi_done, 1)

            def gather_hi(i):
                for q in range(2):
                    act.wait_ge(gather_mm, 2 * i + (q + 1))
                    nc.scalar.copy(ihi[:, 4 * q:4 * q + 4, :], psY[:, 2 + q, :]).then_inc(ihi_done, 1)

            def hidden_hi(i, c):
                act.wait_ge(m_hidT, i * NE + (c + 1))
                nc.scalar.copy(hhi[:, :, 0:P], psB[:, 1, :].rearrange("p (b t) -> p b t", t=P)).then_inc(m_hhi, 1)

            n = n_items(act)
            item_split(0, 0, AHEAD)
            gather_hi(0)
            with act.Fori(0, n) as i:
                done = AHEAD
                for c in range(NE):
                    stop = GS * (item_slot["gate", c] + 1) + AHEAD
                    item_split(i, done, stop)
                    done = stop
                    if c:
                        hidden_hi(i, c - 1)
                    act.wait_ge(group_used, used_at(i, stop - AHEAD))
                    nc.scalar.activation(hid[:, 0, :], psA[:, 0, :], ACT.Silu).then_inc(m_silu, 1)
                stop = GS * item_slot["down", NE - 1] + AHEAD
                item_split(i, done, stop)
                hidden_hi(i, NE - 1)
                gather_hi(i + 1)
                item_split(i, stop, IG)
                item_split(i + 1, 0, AHEAD)
                act.wait_ge(group_used, used_at(i, IG))
                act.wait_ge(pickT_set, 2 * i + 2)
                nc.scalar.activation(yhi[:, :], psY[:, 0:2, :].rearrange("p b n -> p (b n)"), ACT.Copy,
                                     scale=gate_of_slot[:, 0:1]).then_inc(yhi_done, 1)
            act.dma_start(gain, final_norm.partition_broadcast(P)).then_inc(gain_in, 16)
            square_sums(4, lambda tb: (add_done, n * TB + (tb + 1)))

        @block.gpsimd
        def _(pool):
            links = [0]

            def link(ins):
                links[0] += 1
                ins.then_inc(chain_pool, 1)
                pool.wait_ge(chain_pool, links[0])

            def select(ap, fill, op, base, pattern, per_row):
                return nc.gpsimd.affine_select(out=ap, in_=ap, compare_op=op, fill=fill, base=base,
                                               pattern=pattern, channel_multiplier=per_row)

            nc.gpsimd.memset(halfneg[:, :], -0.5)
            link(nc.gpsimd.memset(ident[:, :], 0.0))
            link(select(ident[:, :], 1.0, ALU.not_equal, 0, [[-1, P]], 1))
            nc.gpsimd.memset(ones[:, :], 1.0)
            link(nc.gpsimd.memset(before[:, :], 1.0))
            link(select(before[:, :], 0.0, ALU.is_gt, 0, [[1, P]], -1))
            nc.gpsimd.iota(slotno[:, :], pattern=[[1, P]], base=0, channel_multiplier=0,
                           allow_small_or_imprecise_dtypes=True)
            nc.gpsimd.iota(expert_no[:, :], pattern=[[1, E]], base=0, channel_multiplier=0,
                           allow_small_or_imprecise_dtypes=True)
            nc.gpsimd.iota(dist[:, 0:P], pattern=[[-1, P]], base=0, channel_multiplier=1,
                           allow_small_or_imprecise_dtypes=True)
            link(nc.gpsimd.iota(dist[:, P:3 * P], pattern=[[-1, T]], base=P, channel_multiplier=1,
                                allow_small_or_imprecise_dtypes=True))
            link(select(dist[:, 0:P], BIG, ALU.is_ge, 0, [[-1, P]], 1))
            select(dist[:, P:3 * P], BIG, ALU.is_ge, P, [[-1, T]], 1).then_inc(consts, 1)

            halved = [0]

            def halve_to(n):
                for m in range(halved[0], min(n, NG)):
                    if by_pool[m]:
                        s, g = group_of[m]
                        pool.wait_ge(hi_done, m + 1)
                        nc.gpsimd.tensor_tensor(wlo[:, m % HL, :], ring_group(s, g), f(whi[:, m % HL, :]),
                                                ALU.subtract).then_inc(lo_pool, 1)
                halved[0] = max(halved[0], min(n, NG))

            def root(norm):
                for tb in range(TB):
                    pool.wait_ge(ssq_done, TB * norm + tb + 1)
                    at = rstd[:, norm, tb:tb + 1]
                    link(nc.gpsimd.tensor_scalar(at, ssq[:, norm, tb:tb + 1], 1.0 / D, EPS, ALU.mult, ALU.add))
                    nc.gpsimd.tensor_tensor(at, at, halfneg[:, 0:1], ALU.pow).then_inc(rstd_done, 1)

            root(0)
            halve_to(first_group[first_slot["wo", 0]] + HL)
            for half in range(2):
                pool.wait_ge(o_ssq, (half + 1) * UNITS // 2)
                at = head_rstd[:, half, :]
                link(nc.gpsimd.tensor_scalar(at, head_ssq[:, half, :], 1.0 / P, SUB_EPS, ALU.mult, ALU.add))
                nc.gpsimd.tensor_tensor(at, at, halfneg[:, 0:PAIRS], ALU.pow).then_inc(o_rstd, 1)
            halve_to(first_group[first_slot["ffn", 0]] + HL)
            root(1)
            halve_to(first_group[first_slot["qkv", 1]] + HL)
            root(2)
            halve_to(NG)
            root(3)
            nc.gpsimd.memset(f(pickT[:, :]), 0.0)
            nc.gpsimd.memset(f(yhi[:, :]), 0.0)
            nc.gpsimd.memset(f(ylo[:, :]), 0.0).then_inc(ylo_done, 1)
            n = n_items(pool)
            with pool.Fori(0, n) as i:
                for m in range(POOL_EVERY - 1, IG, POOL_EVERY):
                    j, g = m // GS, m % GS
                    pool.wait_ge(hi_done, used_at(i, m + 1))
                    nc.gpsimd.tensor_tensor(wlo[:, (NG + m) % HL, :], ring[:, (NS + j) % RING, g * GROUP:(g + 1) * GROUP],
                                            f(whi[:, (NG + m) % HL, :]), ALU.subtract).then_inc(lo_pool, 1)
            root(4)

        @block.vector
        def _(dve):
            links = [0]

            def link(ins):
                links[0] += 1
                ins.then_inc(chain_dve, 1)
                dve.wait_ge(chain_dve, links[0])

            halved = [0]

            def halve_to(n):
                for m in range(halved[0], min(n, NG)):
                    if not by_pool[m]:
                        s, g = group_of[m]
                        dve.wait_ge(hi_done, m + 1)
                        nc.vector.tensor_tensor(wlo[:, m % HL, :], ring_group(s, g), f(whi[:, m % HL, :]),
                                                ALU.subtract).then_inc(lo_dve, 1)
                halved[0] = max(halved[0], min(n, NG))

            def norm_rows(norm):
                for tb in range(TB):
                    dve.wait_ge(rstd_done, TB * norm + tb + 1)
                    nc.vector.tensor_scalar(rowbuf[:, tb, :], res[:, tb, :], rstd[:, norm, tb:tb + 1], None,
                                            ALU.mult).then_inc(rows_done, 1)

            def build(b):
                kind, j = BUILDS[b]
                for q in range(KD // 2):
                    dve.wait_ge(xhi_done, 4 * b + q + 1)
                    if kind == "norm":
                        for k in range(2 * q, 2 * q + 2):
                            col = (0, KD, 2 * KD, 3 * KD)[j] + k
                            ins = nc.vector.scalar_tensor_tensor(
                                out=xlo[:, k, :], in0=psY[:, q, (k % 2) * T:(k % 2 + 1) * T],
                                scalar=gain_cols[:, col:col + 1], in1=f(xhi[:, k, :]), op0=ALU.mult, op1=ALU.subtract)
                    else:
                        hi = f(xhi[:, 2 * q:2 * q + 2, :]).rearrange("p k t -> p (k t)")
                        lo = xlo[:, 2 * q:2 * q + 2, :].rearrange("p k t -> p (k t)")
                        if j == 0:
                            ins = nc.vector.scalar_tensor_tensor(
                                out=lo, in0=psY[:, q, :], scalar=gain_cols[:, 4 * KD:4 * KD + 1], in1=hi,
                                op0=ALU.mult, op1=ALU.subtract)
                        else:
                            ins = nc.vector.tensor_tensor(lo, psY[:, q, :], hi, ALU.subtract)
                    ins.then_inc(xlo_done, 1)

            def minima(layer, u):
                n = UNITS * layer + u
                keys = (u % TB + 1) * P
                d = dist[:, 0:P] if u % TB == 0 else dist[:, P:3 * P]
                dve.wait_ge(score_done, n + 1)
                for i in range(2):
                    s = psY[:, 2 * (u % 2) + i, 0:keys]
                    ins = nc.vector.tensor_tensor_reduce(
                        out=s, in0=s, in1=d, scale=slopes[layer][2 * (u // TB) + i], scalar=3e38, op0=ALU.add,
                        op1=ALU.min, accum_out=score_min[:, layer, u, i:i + 1])
                ins.then_inc(min_done, 1)

            def combine(u):
                keys = (u % TB + 1) * P
                dve.wait_ge(exp_done, u + 1)
                link(nc.vector.reciprocal(prob_inv[:, 0, u, :], prob_sum[:, 0, u, :]))
                link(nc.vector.tensor_scalar(mix[:, u:u + 1], prob_sum[:, 0, u, 0:1], prob_inv[:, 0, u, 1:2],
                                             small[:, 4:5], ALU.mult, ALU.mult))
                nc.vector.scalar_tensor_tensor(
                    out=probs[:, u % 2, 0, 0:keys], in0=probs[:, u % 2, 1, 0:keys], scalar=mix[:, u:u + 1],
                    in1=probs[:, u % 2, 0, 0:keys], op0=ALU.mult, op1=ALU.add).then_inc(mixed, 1)

            def invert_and_copy(u):
                blocks = 2 * (u % TB + 1)
                dve.wait_ge(exp_done, UNITS + u + 1)
                nc.vector.reciprocal(prob_inv[:, 1, u, :], prob_sum[:, 1, u, :]).then_inc(mixed, 1)
                dve.wait_ge(probT_done, UNITS + u + 1)
                if u >= 2:
                    dve.wait_ge(pv_done, UNITS + u - 1)
                nc.vector.tensor_copy(probsT[:, u % 2, 0:blocks, :],
                                      psA[:, u % 2, 0:blocks * P]).then_inc(probT_out, 1)

            def output_rows(layer, u):
                pair, tb = u // TB, u % TB
                dve.wait_ge(pv_done, UNITS * layer + u + 1)
                rows_ = rowbuf[:, tb, pair * P:(pair + 1) * P]
                if layer == 0:
                    nc.vector.tensor_scalar(rows_, psB[:, u % 2, 0:P], prob_inv[:, 0, u, 0:1], None,
                                            ALU.mult).then_inc(o_done, 1)
                    dve.wait_ge(o_done, u + 1)
                    nc.vector.tensor_tensor_reduce(
                        out=junk[:, :], in0=rows_, in1=rows_, scale=1.0, scalar=0.0, op0=ALU.mult, op1=ALU.add,
                        accum_out=head_ssq[:, u // (UNITS // 2), u % (UNITS // 2):u % (UNITS // 2) + 1]).then_inc(o_ssq, 1)
                else:
                    dve.wait_ge(mixed, UNITS + u + 1)
                    for i in range(2):
                        ins = nc.vector.tensor_scalar(rows_[:, 64 * i:64 * i + 64], psB[:, u % 2, 64 * i:64 * i + 64],
                                                      prob_inv[:, 1, u, i:i + 1], None, ALU.mult)
                    ins.then_inc(o_done, 1)

            def add_to_residual(tb, ps):
                r = res[:, tb, :]
                return nc.vector.tensor_tensor(r, ps.rearrange("p b n -> p (b n)"), r, ALU.add)

            for layer in range(2):
                for pair in range(PAIRS):
                    for i in range(2):
                        nc.vector.memset(q_scale[64 * i:64 * i + 64, layer, pair:pair + 1],
                                         -SCALE / slopes[layer][2 * pair + i])
            dve.wait_ge(small_in, 16 * 6)
            for i in range(2):
                ins = nc.vector.tensor_tensor_reduce(
                    out=lam_prod, in0=lam[:, 2 * i, :], in1=lam[:, 2 * i + 1, :], scale=1.0, scalar=0.0,
                    op0=ALU.mult, op1=ALU.add, accum_out=small[:, i:i + 1])
                if i == 0:
                    link(ins)
            ins.then_inc(lam_dot, 1)
            halve_to(HL)
            dve.wait_ge(gains_T, 1)
            nc.vector.tensor_copy(gain_cols[:, 0:4 * KD], psA[:, 0, 0:4 * KD])
            nc.vector.tensor_scalar(gain_cols[:, 4 * KD:4 * KD + 1], psA[:, 0, 4 * KD:4 * KD + 1], SUB, None,
                                    ALU.mult).then_inc(gains_set, 1)
            norm_rows(0)
            dve.wait_ge(lam_exp, 1)
            link(nc.vector.tensor_tensor(small[:, 5:6], small[:, 3:4], small[:, 2:3], ALU.subtract))
            link(nc.vector.tensor_scalar(small[:, 4:5], small[:, 5:6], -LAM_INIT, None, ALU.add))
            for layer in range(2):
                build(3 * layer)
                halve_to(first_group[first_slot["wo", layer]] + HL)
                if layer == 0:
                    dve.wait_ge(consts, 1)
                for u in range(UNITS + 2):
                    if u < UNITS:
                        minima(layer, u)
                    if 1 <= u <= UNITS:
                        if layer == 0:
                            combine(u - 1)
                        else:
                            invert_and_copy(u - 1)
                    if u >= 2:
                        output_rows(layer, u - 2)
                    if layer == 0 and u in (UNITS // 2 + 1, UNITS + 1):
                        half = 0 if u < UNITS else 1
                        dve.wait_ge(o_rstd, half + 1)
                        for m in range(half * UNITS // 2, (half + 1) * UNITS // 2):
                            pair, tb = m // TB, m % TB
                            rows_ = rowbuf[:, tb, pair * P:(pair + 1) * P]
                            ins = nc.vector.tensor_scalar(
                                rows_, rows_, head_rstd[:, half, m % (UNITS // 2):m % (UNITS // 2) + 1], None, ALU.mult)
                        ins.then_inc(rows_done, 1)
                build(3 * layer + 1)
                end = first_group[first_slot["wo", layer] + 2]
                halve_to(end + HL)
                dve.wait_ge(group_used, end)
                for tb, ps in enumerate((psA, psB)):
                    add_to_residual(tb, ps[:, :, :]).then_inc(res_done, 1)
                if layer == 1:
                    break
                norm_rows(1)
                build(2)
                for c in range(NF):
                    w = width[c]
                    halve_to(first_group[up_slot[c] + 1] + AHEAD)
                    dve.wait_ge(silu_done, c + 1)
                    dve.wait_ge(group_used, first_group[up_slot[c] + 1])
                    nc.vector.tensor_tensor(hid[:, :, 0:w], psB[:, :, 0:w], hid[:, :, 0:w], ALU.mult).then_inc(hid_done, 1)
                    last = down_slot[c - 1] if c else up_slot[c]
                    halve_to(first_group[last + 1] + AHEAD)
                    for q in range(w // (2 * P)):
                        dve.wait_ge(hhi_done, 2 * c + q + 1)
                        nc.vector.tensor_tensor(
                            hlo[:, 2 * q:2 * q + 2, :].rearrange("p k t -> p (k t)"), psB[:, q, :],
                            f(hhi[:, 2 * q:2 * q + 2, :]).rearrange("p k t -> p (k t)"), ALU.subtract).then_inc(hlo_done, 1)
                end = first_group[first_slot["qkv", 1]]
                halve_to(end + HL)
                dve.wait_ge(group_used, end)
                for tb in range(TB):
                    add_to_residual(tb, psY[:, 2 * tb:2 * tb + 2, :]).then_inc(res_done, 1)
                norm_rows(2)

            dve.wait_ge(rt_split, 1)
            nc.vector.tensor_tensor(rt_lo[:, :, :], rt[:, :, :], f(rt_hi[:, :, :]), ALU.subtract).then_inc(rt_split, 1)
            norm_rows(3)
            build(5)
            dve.wait_ge(gain_in, 16)
            for tb in range(TB):
                ins = nc.vector.tensor_tensor(rowbuf[:, tb, :], rowbuf[:, tb, :], gain, ALU.mult)
            ins.then_inc(rows_done, 1)
            dve.wait_ge(logit_mm, 1)
            link(nc.vector.tensor_copy(logit[:, :, :], psA[:, 0, 0:TB * E].rearrange("p (b e) -> p b e", e=E)))
            for tb in range(TB):
                link(nc.vector.max(top[:, tb, :], logit[:, tb, :]))
            for tb in range(TB):
                link(nc.vector.max_index(top_at[:, tb, :], top[:, tb, :], logit[:, tb, :]))
            nc.vector.tensor_tensor(wtmp[:, 1, :], top[:, :, 1], top[:, :, 0], ALU.subtract).then_inc(wdiff, 1)
            link(nc.vector.tensor_copy(top_atf[:, :, :], top_at[:, :, :]))
            for tb in range(TB):
                nc.vector.tensor_scalar(isA[:, tb, :], expert_no[:, :], top_atf[:, tb, 0:1], None, ALU.is_equal)
                ins = nc.vector.tensor_scalar(isB[:, tb, :], expert_no[:, :], top_atf[:, tb, 1:2], None, ALU.is_equal)
            link(ins)
            nc.vector.tensor_tensor(member[:, :, :], isA[:, :, :], isB[:, :, :], ALU.add).then_inc(member_set, 1)
            dve.wait_ge(wexp, 1)
            link(nc.vector.tensor_scalar(wtmp[:, 1, :], wtmp[:, 0, :], 1.0, None, ALU.add))
            link(nc.vector.reciprocal(wgt[:, 0, :], wtmp[:, 1, :]))
            link(nc.vector.tensor_tensor(wgt[:, 1, :], wgt[:, 0, :], wtmp[:, 0, :], ALU.mult))
            dve.wait_ge(pos_mm, 1)
            link(nc.vector.tensor_copy(pos[:, :, :], psA[:, 1, 0:3 * E].rearrange("p (b e) -> p b e", e=E)))
            link(nc.vector.tensor_scalar(over[:, :], pos[:, 2, :], float(P), None, ALU.is_gt))
            link(nc.vector.memset(over_before[:, :], 0.0))
            for e in range(1, E):
                link(nc.vector.tensor_tensor(over_before[:, e:e + 1], over_before[:, e - 1:e], over[:, e - 1:e], ALU.add))
            link(nc.vector.tensor_tensor(extra_f[:, 0:1], over_before[:, E - 1:E], over[:, E - 1:E], ALU.add))
            for k in range(3):
                link(nc.vector.tensor_scalar(far[:, 0, :], over_before[:, :], float(k), None, ALU.is_equal))
                link(nc.vector.tensor_tensor(far[:, 0, :], far[:, 0, :], over[:, :], ALU.mult))
                link(nc.vector.tensor_tensor_reduce(
                    out=far[:, 1, :], in0=far[:, 0, :], in1=expert_no[:, :], scale=1.0, scalar=0.0, op0=ALU.mult,
                    op1=ALU.add, accum_out=extra_f[:, k + 1:k + 2]))
            nc.vector.tensor_copy(extra[:, :], extra_f[:, :]).then_inc(table_set, 1)
            link(nc.vector.tensor_tensor(jump[:, :], over_before[:, :], expert_no[:, :], ALU.subtract))
            link(nc.vector.tensor_scalar(jump[:, :], jump[:, :], float(P), float(P * (E - 1)), ALU.mult, ALU.add))
            for tb in range(TB):
                link(nc.vector.tensor_scalar(far[:, tb, :], pos[:, tb, :], float(P), None, ALU.is_ge))
                link(nc.vector.tensor_tensor(far[:, tb, :], far[:, tb, :], jump[:, :], ALU.mult))
                link(nc.vector.scalar_tensor_tensor(out=place[:, tb, :], in0=expert_no[:, :], scalar=float(P),
                                                    in1=pos[:, tb, :], op0=ALU.mult, op1=ALU.add))
                link(nc.vector.tensor_tensor(place[:, tb, :], place[:, tb, :], far[:, tb, :], ALU.add))
                for a, chosen in enumerate((isA, isB)):
                    link(nc.vector.tensor_tensor_reduce(
                        out=tmpE[:, tb, :], in0=place[:, tb, :], in1=chosen[:, tb, :], scale=1.0, scalar=0.0,
                        op0=ALU.mult, op1=ALU.add, accum_out=key[:, a, tb:tb + 1]))
            dve.wait_ge(rowsplit, 1)
            nc.vector.tensor_tensor(xlo[:, :, :].rearrange("p k t -> p (k t)"), rowbuf[:, :, :].rearrange("p b d -> p (b d)"),
                                    f(xhi[:, :, :]).rearrange("p k t -> p (k t)"), ALU.subtract).then_inc(rowsplit, 1)

            def one_hots(i):
                for tb in range(TB):
                    ins = nc.vector.tensor_scalar(eqA[:, tb, :], slotno[:, :], key[:, 0, tb:tb + 1], None, ALU.is_equal)
                ins.then_inc(pick_set, 1)
                dve.wait_ge(pick_set, 4 * i + 1)
                for tb in range(TB):
                    ins = nc.vector.scalar_tensor_tensor(
                        out=pick[:, tb, :], in0=slotno[:, :], scalar=key[:, 1, tb:tb + 1], in1=eqA[:, tb, :],
                        op0=ALU.is_equal, op1=ALU.add)
                ins.then_inc(pick_set, 1)
                dve.wait_ge(pick_set, 4 * i + 2)
                for a, eq in enumerate((eqA, eqB)):
                    for tb in range(TB):
                        ins = nc.vector.tensor_scalar(eq[:, tb, :], slotno[:, :], key[:, a, tb:tb + 1], wgt[:, a, tb:tb + 1],
                                                      ALU.is_equal, ALU.mult)
                ins.then_inc(pick_set, 1)
                dve.wait_ge(pick_set, 4 * i + 3)
                nc.vector.tensor_scalar(key[:, :, :], key[:, :, :], -float(P), None, ALU.add).then_inc(pick_set, 1)
                dve.wait_ge(pick_set, 4 * i + 4)

            def item_halve(i, first, last):
                for m in range(first, last):
                    if m % POOL_EVERY != POOL_EVERY - 1:
                        dve.wait_ge(hi_done, used_at(i, m + 1))
                        g = m % GS
                        nc.vector.tensor_tensor(
                            wlo[:, (NG + m) % HL, :], ring[:, (NS + m // GS) % RING, g * GROUP:(g + 1) * GROUP],
                            f(whi[:, (NG + m) % HL, :]), ALU.subtract).then_inc(lo_dve, 1)

            def gather_lo(i):
                for q in range(2):
                    dve.wait_ge(ihi_done, 2 * i + (q + 1))
                    nc.vector.tensor_tensor(
                        ilo[:, 4 * q:4 * q + 4, :].rearrange("p k t -> p (k t)"), psY[:, 2 + q, :],
                        f(ihi[:, 4 * q:4 * q + 4, :]).rearrange("p k t -> p (k t)"), ALU.subtract).then_inc(ilo_done, 1)

            def hidden_lo(i, c):
                dve.wait_ge(m_hhi, i * NE + (c + 1))
                nc.vector.tensor_tensor(hlo[:, :, 0:P], psB[:, 1, :].rearrange("p (b t) -> p b t", t=P),
                                        f(hhi[:, :, 0:P]), ALU.subtract).then_inc(m_hlo, 1)

            def add_scattered(i, tb):
                dve.wait_ge(scatter_mm, TB * i + (tb + 1))
                add_to_residual(tb, psY[:, 2:4, :]).then_inc(add_done, 1)

            one_hots(0)
            n = n_items(dve)
            item_halve(0, 0, AHEAD)
            gather_lo(0)
            with dve.Fori(0, n) as i:
                done = AHEAD
                for c in range(NE):
                    stop = GS * (item_slot["gate", c] + 1) + AHEAD
                    item_halve(i, done, stop)
                    if c == 0:
                        add_scattered(i, 0)
                    else:
                        hidden_lo(i, c - 1)
                    done, stop = stop, GS * (item_slot["up", c] + 1) + AHEAD
                    item_halve(i, done, stop)
                    done = stop
                    dve.wait_ge(m_silu, i * NE + (c + 1))
                    dve.wait_ge(group_used, used_at(i, stop - AHEAD))
                    nc.vector.tensor_tensor(hid[:, 0, :], psB[:, 0, :], hid[:, 0, :], ALU.mult).then_inc(m_hid, 1)
                    if c == 0:
                        add_scattered(i, 1)
                    if c == 1:
                        dve.wait_ge(pickT_mm, i + 1)
                        nc.vector.tensor_copy(pickT[:, :], psA[:, 1, 0:T]).then_inc(pickT_set, 1)
                        nc.vector.tensor_copy(gate_of_slot[:, :], psA[:, 1, T:T + 1]).then_inc(pickT_set, 1)
                        one_hots(i + 1)
                stop = GS * item_slot["down", NE - 1] + AHEAD
                item_halve(i, done, stop)
                hidden_lo(i, NE - 1)
                gather_lo(i + 1)
                item_halve(i, stop, IG)
                item_halve(i + 1, 0, AHEAD)
                dve.wait_ge(yhi_done, i + 1)
                nc.vector.scalar_tensor_tensor(out=ylo[:, :], in0=psY[:, 0:2, :].rearrange("p b n -> p (b n)"),
                                               scalar=gate_of_slot[:, 0:1], in1=f(yhi[:, :]), op0=ALU.mult,
                                               op1=ALU.subtract).then_inc(ylo_done, 1)
            for tb in range(TB):
                add_scattered(n, tb)
            dve.wait_ge(gain_in, 32)
            for tb in range(TB):
                dve.wait_ge(rstd_done, TB * 4 + tb + 1)
                nc.vector.scalar_tensor_tensor(out=rowbuf[:, tb, :], in0=res[:, tb, :], scalar=rstd[:, 4, tb:tb + 1],
                                               in1=gain, op0=ALU.mult, op1=ALU.mult).then_inc(out_rows, 1)

        @block.tensor
        def _(pe):
            mm = nc.tensor.matmul

            def three(ps, xh, xl, wh, wl, start, stop, shared=False):
                mm(ps, xh, wh, start=start, stop=False, skip_group_check=shared)
                mm(ps, xh, wl, start=False, stop=False, skip_group_check=shared)
                return mm(ps, xl, wh, start=False, stop=stop, skip_group_check=shared)

            def build(b):
                kind, j = BUILDS[b]
                for q in range(KD // 2):
                    if b == 4:
                        pe.wait_ge(o_done, UNITS + (q // 2 + 1) * UNITS // 2)
                    elif kind == "attn":
                        pe.wait_ge(rows_done, ROWS_BEFORE[b] + q // 2 + 1)
                    for tb in range(TB):
                        if kind == "norm" and q == 0:
                            pe.wait_ge(rows_done, ROWS_BEFORE[b] + tb + 1)
                        for k in range(2):
                            ins = nc.tensor.transpose(psY[:, q, k * T + tb * P:k * T + (tb + 1) * P],
                                                      rowbuf[:, tb, (2 * q + k) * P:(2 * q + k + 1) * P], ident[:, :])
                    ins.then_inc(turn_done, 1)

            def cols_slot(s, b, ps, w=W):
                per = GROUP // w
                for g in range(slots[s][1]):
                    n = first_group[s] + g
                    wait_group(pe, n)
                    for kk in range(per):
                        k = per * g + kk
                        if k % 2 == 0:
                            pe.wait_ge(xlo_done, 4 * b + k // 2 + 1)
                        for tb in range(TB):
                            xs = slice(tb * P, (tb + 1) * P)
                            ws = slice(kk * w, (kk + 1) * w)
                            ins = three(ps[:, tb, 0:w], xhi[:, k, xs], xlo[:, k, xs], whi[:, n % HL, ws],
                                        wlo[:, n % HL, ws], k == 0, k == KD - 1)
                    ins.then_inc(group_used, 1)

            def turned_slot(s, b, ps):
                for k in range(KD):
                    n = first_group[s] + k
                    wait_group(pe, n)
                    pe.wait_ge(xlo_done, 4 * b + k // 2 + 1)
                    for fb in range(4):
                        ws = slice(fb * P, (fb + 1) * P)
                        ins = three(ps[:, fb // 2, (fb % 2) * T:(fb % 2 + 1) * T], whi[:, n % HL, ws],
                                    wlo[:, n % HL, ws], xhi[:, k, :], xlo[:, k, :],
                                    k == 0 and fb % 2 == 0, k == KD - 1, shared=True)
                    ins.then_inc(group_used, 1)

            def rows_slot(s, left, outs, first, last):
                for g in range(slots[s][1]):
                    n, (k, half) = first_group[s] + g, divmod(g, 2)
                    wait_group(pe, n)
                    xh, xl = left(k)
                    for tb in range(TB):
                        xs = slice(tb * P, (tb + 1) * P)
                        ins = three(outs[tb][:, half, :], xh[:, xs], xl[:, xs], whi[:, n % HL, :],
                                    wlo[:, n % HL, :], first and k == 0, last and g >= slots[s][1] - 2)
                    ins.then_inc(group_used, 1)

            def scores(layer, u):
                n, pair, tb = UNITS * layer + u, u // TB, u % TB
                keys = (tb + 1) * P
                pe.wait_ge(qkv_done, 6 * layer + (2 if pair < 4 else 4))
                if u >= 2:
                    pe.wait_ge(exp_done, n - 1)
                for i in range(2):
                    rows_ = slice(64 * i, 64 * i + 64)
                    ins = mm(psY[:, 2 * (u % 2) + i, 0:keys], qT[rows_, pair, tb * P:(tb + 1) * P],
                             kT[rows_, pair, 0:keys], start=True, stop=True)
                ins.then_inc(score_done, 1)

            def turn_probs(layer, u):
                n, tb = UNITS * layer + u, u % TB
                if layer == 0:
                    pe.wait_ge(mixed, u + 1)
                else:
                    pe.wait_ge(exp_done, n + 1)
                if u >= 2:
                    pe.wait_ge(probT_out, n - 1)
                else:
                    pe.wait_ge(qkv_done, 6 * layer + 5)
                at = 0
                for i in range(1 if layer == 0 else 2):
                    for kb in range(tb + 1):
                        ins = nc.tensor.transpose(psA[:, u % 2, at * P:(at + 1) * P],
                                                  probs[:, u % 2, i, kb * P:(kb + 1) * P], ident[:, :])
                        at += 1
                ins.then_inc(probT_done, 1)

            def weigh_values(layer, u):
                n, pair, tb = UNITS * layer + u, u // TB, u % TB
                pe.wait_ge(probT_out, n + 1)
                if u >= 2:
                    pe.wait_ge(o_done, n - 1)
                else:
                    pe.wait_ge(qkv_done, 6 * layer + 6)
                heads = 1 if layer == 0 else 2
                wide = P // heads
                for i in range(heads):
                    for kb in range(tb + 1):
                        c = pair * P + i * wide
                        ins = mm(psB[:, u % 2, i * wide:(i + 1) * wide], probsT[:, u % 2, i * (tb + 1) + kb, :],
                                 val[:, kb, c:c + wide], start=kb == 0, stop=kb == tb)
                ins.then_inc(pv_done, 1)

            pe.wait_ge(consts, 1)
            pe.wait_ge(small_in, 16 * 6)
            nc.tensor.transpose(psA[:, 0, 0:4 * KD + 1], gain_rows[0:4 * KD + 1, :],
                                ident[0:4 * KD + 1, 0:4 * KD + 1]).then_inc(gains_T, 1)
            for layer in range(2):
                b = 3 * layer
                build(b)
                s0 = first_slot["qkv", layer]
                for j in range(6):
                    if j >= 2:
                        pe.wait_ge(qkv_done, 6 * layer + j - 1)
                    elif layer == 0:
                        pe.wait_ge(gains_set, 1)
                    (turned_slot if j < 4 else cols_slot)(s0 + j, b, psA if j % 2 == 0 else psB)
                for u in range(UNITS + 2):
                    if u < UNITS:
                        scores(layer, u)
                    if 1 <= u <= UNITS:
                        turn_probs(layer, u - 1)
                    if u >= 2:
                        weigh_values(layer, u - 2)
                build(b + 1)
                pe.wait_ge(o_done, UNITS * (layer + 1))
                for j in range(2):
                    def attn_left(g, j=j):
                        k = 4 * j + g
                        pe.wait_ge(xlo_done, 4 * (b + 1) + k // 2 + 1)
                        return xhi[:, k, :], xlo[:, k, :]
                    rows_slot(first_slot["wo", layer] + j, attn_left, (psA, psB), j == 0, j == 1)
                if layer == 1:
                    break
                build(2)
                for c in range(NF + 1):
                    if c < NF:
                        if c:
                            pe.wait_ge(silu_done, c)
                        cols_slot(gate_slot[c], 2, psA, width[c])
                        if c:
                            pe.wait_ge(hlo_done, 2 * c)
                        cols_slot(up_slot[c], 2, psB, width[c])
                    if c:
                        def hidden_left(g, c=c):
                            pe.wait_ge(hlo_done, 2 * (c - 1) + g // 2 + 1)
                            return hhi[:, g, :], hlo[:, g, :]
                        rows_slot(down_slot[c - 1], hidden_left, (psY[:, 0:2, :], psY[:, 2:4, :]), c == 1, c == NF)
                    if c < NF:
                        pe.wait_ge(hid_done, c + 1)
                        for q in range(width[c] // (2 * P)):
                            for fb in range(2):
                                for tb in range(TB):
                                    ins = nc.tensor.transpose(
                                        psB[:, q, fb * T + tb * P:fb * T + (tb + 1) * P],
                                        hid[:, tb, (2 * q + fb) * P:(2 * q + fb + 1) * P], ident[:, :])
                            ins.then_inc(hidT_done, 1)

            build(5)
            pe.wait_ge(rt_split, 2)
            for tb in range(TB):
                for k in range(KD):
                    pe.wait_ge(xlo_done, 4 * 5 + k // 2 + 1)
                    xs = slice(tb * P, (tb + 1) * P)
                    ins = three(psA[:, 0, tb * E:(tb + 1) * E], xhi[:, k, xs], xlo[:, k, xs], rt_hi[:, k, :],
                                rt_lo[:, k, :], k == 0, k == KD - 1)
            ins.then_inc(logit_mm, 1)
            pe.wait_ge(member_set, 1)
            mm(psA[:, 1, 0:E], before[:, :], member[:, 0, :], start=True, stop=True)
            mm(psA[:, 1, E:2 * E], before[:, :], member[:, 1, :], start=True, stop=False)
            mm(psA[:, 1, E:2 * E], ones[:, :], member[:, 0, :], start=False, stop=True)
            mm(psA[:, 1, 2 * E:3 * E], ones[:, :], member[:, 0, :], start=True, stop=False)
            mm(psA[:, 1, 2 * E:3 * E], ones[:, :], member[:, 1, :], start=False, stop=True).then_inc(pos_mm, 1)

            rows_hi = xhi[:, :, :].rearrange("p k t -> p (k t)")
            rows_lo = xlo[:, :, :].rearrange("p k t -> p (k t)")

            def gather(i):
                pe.wait_ge(pick_set, 4 * i + 2)
                for q in range(2):
                    for k in range(4 * q, 4 * q + 4):
                        for tb in range(TB):
                            for part, rows_ in enumerate((rows_hi, rows_lo)):
                                ins = mm(psY[:, 2 + q, (k % 4) * P:(k % 4 + 1) * P],
                                         rows_[:, tb * D + k * P:tb * D + (k + 1) * P], pick[:, tb, :],
                                         start=tb == 0 and part == 0, stop=tb == TB - 1 and part == 1)
                    ins.then_inc(gather_mm, 1)

            def scatter(i, tb):
                if tb == 0:
                    pe.wait_ge(ylo_done, i + 1)
                    pe.wait_ge(ilo_done, 2 * i + 2)
                else:
                    pe.wait_ge(add_done, TB * i + tb)
                for half in range(2):
                    ws = slice(half * W, (half + 1) * W)
                    mm(psY[:, 2 + half, :], pickT[:, tb * P:(tb + 1) * P], yhi[:, ws], start=True, stop=False)
                    ins = mm(psY[:, 2 + half, :], pickT[:, tb * P:(tb + 1) * P], ylo[:, ws], start=False, stop=True)
                ins.then_inc(scatter_mm, 1)

            def hidden_turn(i, c):
                pe.wait_ge(m_hid, i * NE + (c + 1))
                for fb in range(FBW):
                    ins = nc.tensor.transpose(psB[:, 1, fb * P:(fb + 1) * P], hid[:, 0, fb * P:(fb + 1) * P], ident[:, :])
                ins.then_inc(m_hidT, 1)

            def item_slot_products(i, j):
                kind, c = item_slots[j]
                if kind == "gate" and c:
                    pe.wait_ge(m_silu, i * NE + c)
                if kind == "down":
                    pe.wait_ge(m_hlo, i * NE + (c + 1))
                for g in range(GS):
                    m = GS * j + g
                    at = (NG + m) % HL
                    wait_item_group(pe, i, m)
                    if kind == "down":
                        k, half = divmod(g, 2)
                        ins = three(psY[:, half, :], hhi[:, k, 0:P], hlo[:, k, 0:P], whi[:, at, :], wlo[:, at, :],
                                    c == 0 and k == 0, c == NE - 1 and k == FBW - 1)
                    else:
                        ps = (psA if kind == "gate" else psB)[:, 0, :]
                        ins = three(ps, ihi[:, g, :], ilo[:, g, :], whi[:, at, :], wlo[:, at, :], g == 0, g == KD - 1)
                    ins.then_inc(group_used, 1)

            pe.wait_ge(rowsplit, 2)
            gather(0)
            n = n_items(pe)
            with pe.Fori(0, n) as i:
                pe.wait_ge(ilo_done, 2 * i + 2)
                for j, (kind, c) in enumerate(item_slots):
                    if j == IS - 1:
                        hidden_turn(i, NE - 1)
                        gather(i + 1)
                    item_slot_products(i, j)
                    if kind == "gate" and c == 0:
                        scatter(i, 0)
                    if kind == "up" and c == 0:
                        scatter(i, 1)
                    if kind == "gate" and c:
                        hidden_turn(i, c - 1)
                    if kind == "up" and c == 1:
                        pe.wait_ge(pick_set, 4 * i + 3)
                        for tb in range(TB):
                            nc.tensor.transpose(psA[:, 1, tb * P:(tb + 1) * P], f(pick[:, tb, :]), ident[:, :])
                        for a, eq in enumerate((eqA, eqB)):
                            for tb in range(TB):
                                ins = mm(psA[:, 1, T:T + 1], eq[:, tb, :], ones[:, 0:1], start=a == 0 and tb == 0,
                                         stop=a == 1 and tb == 1)
                        ins.then_inc(pickT_mm, 1)
            for tb in range(TB):
                scatter(n, tb)


_INS = ["x", "norm_mix", "norm_ffn", "diff_w_qkv", "diff_w_o", "diff_lambda", "diff_subln", "moba_w_qkv", "moba_w_o",
        "ffn_w_gate", "ffn_w_up", "ffn_w_down", "moe_router", "moe_w_gate", "moe_w_up", "moe_w_down", "final_norm"]


def kernel(**inputs):
    import concourse.bacc as bacc
    from concourse.bass_utils import run_bass_kernel_spmd

    nc = bacc.Bacc("TRN2", target_bir_lowering=False, num_devices=1)
    arrays, args = {}, []
    for name in _INS:
        a = np.ascontiguousarray(inputs[name])
        arrays[f"in_{name}"] = a
        args.append(nc.dram_tensor(f"in_{name}", a.shape, mybir.dt.from_np(a.dtype), kind="ExternalInput").ap())
    args.append(nc.dram_tensor("out", inputs["x"].shape, F32, kind="ExternalOutput").ap())
    trunk(nc, *args)
    return run_bass_kernel_spmd(nc, [arrays], core_ids=[0]).results[0]["out"]
```

```python
import math
from contextlib import ExitStack

import numpy as np
import concourse.bass as bass
from concourse import mybir

F32 = mybir.dt.float32
F32R = mybir.dt.float32r
I32 = mybir.dt.int32
U32 = mybir.dt.uint32
ALU = mybir.AluOpType
ACT = mybir.ActivationFunctionType
AX = mybir.AxisListType

P = 128
GROUP = 512
RING = 7
HL = 6
AHEAD = 5
GS = 8
SLOT = GS * GROUP
POOL_EVERY = 4
POOL_GS = GS // POOL_EVERY
BIG = 1e30


def trunk(nc, x, norm_mix, norm_ffn, diff_w_qkv, diff_w_o, diff_lambda, diff_subln, moba_w_qkv, moba_w_o,
          ffn_w_gate, ffn_w_up, ffn_w_down, moe_router, moe_w_gate, moe_w_up, moe_w_down, final_norm, out):
    _, T, D = x.shape
    TB = T // P
    KD = D // P
    FF = ffn_w_gate.shape[2]
    E, DE = moe_w_gate.shape[1], moe_w_gate.shape[3]
    W = 512
    NF = -(-FF // W)
    NE = DE // W
    FBW = W // P
    PAIRS = D // P
    UNITS = PAIRS * TB
    EPS, SUB_EPS, SUB = 1e-6, 1e-5, 1.0 - (0.8 - 0.6 * math.exp(0.0))
    LAM_INIT = 0.8 - 0.6 * math.exp(0.0)
    SCALE = 64 ** -0.5
    assert T == 2 * P and D == 1024 and DE % W == 0 and 2 * T // (P + 1) <= 3
    slopes = [[2.0 ** (-8.0 * (p + 1) / PAIRS) for p in range(PAIRS) for _ in range(2)],
              [2.0 ** (-8.0 * (h + 1) / (2 * PAIRS)) for h in range(2 * PAIRS)]]

    slots = []

    def cols(w, k, c, n):
        return w[0].rearrange("(k p) n -> p k n", p=P)[:, :, c:c + n]

    def rows(w, r, n):
        return w[0][r:r + n, :].rearrange("(g p) n -> p g n", p=P)

    first_slot = {}
    for layer, (wqkv, wo) in enumerate(((diff_w_qkv, diff_w_o), (moba_w_qkv, moba_w_o))):
        first_slot["qkv", layer] = len(slots)
        for c in (0, D, 2 * D, W, D + W, 2 * D + W):
            slots.append((cols(wqkv, KD, c, W), GS))
        first_slot["wo", layer] = len(slots)
        for r in (0, W):
            slots.append((rows(wo, r, W), GS))
        if layer == 0:
            first_slot["ffn", 0] = len(slots)
            width = [min(W, FF - c * W) for c in range(NF)]
            gate_slot, up_slot, down_slot = {}, {}, {}
            for c in range(NF + 1):
                if c < NF:
                    gate_slot[c] = len(slots)
                    slots.append((cols(ffn_w_gate, KD, c * W, width[c]), width[c] * KD // GROUP))
                    up_slot[c] = len(slots)
                    slots.append((cols(ffn_w_up, KD, c * W, width[c]), width[c] * KD // GROUP))
                if c > 0:
                    down_slot[c - 1] = len(slots)
                    slots.append((rows(ffn_w_down, (c - 1) * W, width[c - 1]), width[c - 1] // P * D // GROUP))
    NS = len(slots)
    first_group = [sum(g for _, g in slots[:s]) for s in range(NS + 1)]
    NG = first_group[NS]

    STEPS = UNITS + 2
    FILL = ([5, 3, 3, 3, 3, 3, 3, 3, 4, 2, 0, 0, 0, 1, 1, 1, 1, 1], [5, 3, 3, 3, 3, 3, 3, 3, 4, 2, 0, 0, 0, 1, 1, 1, 1, 1])
    HALF_BUILD = 12
    filled = [[first_group[first_slot["qkv", layer] + 2] + sum(FILL[layer][:t]) for t in range(STEPS + 1)]
              for layer in range(2)]
    ends = [[[s for s in range(first_slot["qkv", layer] + 2, first_slot["wo", layer])
              if filled[layer][t] < first_group[s + 1] <= filled[layer][t + 1]] for t in range(STEPS)]
            for layer in range(2)]
    assert all(filled[layer][11] == first_group[first_slot["wo", layer]] for layer in range(2))
    group_of = [(s, g) for s in range(NS) for g in range(slots[s][1])]
    by_pool = [g % POOL_EVERY == POOL_EVERY - 1 for _, g in group_of]
    pool_upto = [sum(by_pool[:n]) for n in range(NG + 1)]
    dve_upto = [n - pool_upto[n] for n in range(NG + 1)]

    item_slots = [("gate", 0), ("up", 0)]
    for c in range(1, NE):
        item_slots += [("gate", c), ("up", c), ("down", c - 1)]
    item_slots += [("down", NE - 1)]
    item_slot = {key: j for j, key in enumerate(item_slots)}
    IS = len(item_slots)
    IG = GS * IS
    assert IS % RING == 0 and IG % HL == 0 and all(g == GS for _, g in slots[-RING:])

    with ExitStack() as ctx:
        def sb(name, shape, dt=F32, stack=ctx):
            return stack.enter_context(nc.sbuf_tensor(name, shape, dt))

        def sem(name):
            return ctx.enter_context(nc.semaphore(name))

        ring = sb("ring", [P, RING, SLOT])
        whi = sb("whi", [P, HL, GROUP], F32R)
        wlo = sb("wlo", [P, HL, GROUP], F32R)
        xhi = sb("xhi", [P, KD, T], F32R)
        xlo = sb("xlo", [P, KD, T], F32R)
        res = sb("res", [P, TB, D])
        rowbuf = sb("rowbuf", [P, TB, D])
        rt = sb("rt", [P, KD, E])
        expert_no = sb("expert_no", [P, E])
        ident = sb("ident", [P, P])
        ones = sb("ones", [P, P])
        before = sb("before", [P, P])
        slotno = sb("slotno", [P, P])
        gain_rows = sb("gain_rows", [40, P])
        gain_cols = sb("gain_cols", [P, 40])
        small = sb("small", [P, 16])
        ssq = sb("ssq", [P, 5, TB])
        rstd = sb("rstd", [P, 5, TB])
        q_scale = sb("q_scale", [P, 2, PAIRS])
        halfneg = sb("halfneg", [P, 2 * PAIRS])
        score_min = sb("score_min", [P, 2, UNITS, 2])
        prob_sum = sb("prob_sum", [P, 2, UNITS, 2])
        prob_inv = sb("prob_inv", [P, 2, UNITS, 2])
        mix = sb("mix", [P, UNITS])
        head_ssq = sb("head_ssq", [P, TB, PAIRS])
        head_rstd = sb("head_rstd", [P, TB, PAIRS])

        attn = ExitStack()
        qT = sb("qT", [P, PAIRS, T], F32, attn)
        kT = sb("kT", [P, PAIRS, T], F32, attn)
        val = sb("val", [P, TB, D], F32, attn)
        probs = sb("probs", [P, 2, 2, T], F32, attn)
        lam = probs[:, 0, 0, :].rearrange("p (a d) -> p a d", a=4)
        lam_prod = probs[:, 0, 1, 0:64]
        junk = sb("junk", [P, P], F32, attn)
        probsT = sb("probsT", [P, 2, 4, P], F32, attn)
        dist = sb("dist", [P, 3 * P], F32, attn)
        attn.close()
        hid = sb("hid", [P, TB, W])
        gain = hid[:, :, :].rearrange("p b n -> p (b n)")
        hhi = sb("hhi", [P, FBW, T], F32R)
        hlo = sb("hlo", [P, FBW, T], F32R)
        ihi = sb("ihi", [P, KD, P], F32R)
        ilo = sb("ilo", [P, KD, P], F32R)
        yhi = sb("yhi", [P, D], F32R)
        ylo = sb("ylo", [P, D], F32R)
        pick = sb("pick", [P, TB, P], F32R)
        pickT = sb("pickT", [P, T], F32R)
        eqA = sb("eqA", [P, TB, P])
        eqB = sb("eqB", [P, TB, P])
        gate_of_slot = sb("gate_of_slot", [P, 1])
        rt_hi = sb("rt_hi", [P, KD, E], F32R)
        rt_lo = sb("rt_lo", [P, KD, E], F32R)
        logit = sb("logit", [P, TB, E])
        top = sb("top", [P, TB, E])
        top_at = sb("top_at", [P, TB, E], U32)
        top_atf = sb("top_atf", [P, TB, E])
        isA = sb("isA", [P, TB, E])
        isB = sb("isB", [P, TB, E])
        member = sb("member", [P, TB, E])
        pos = sb("pos", [P, 3, E])
        over = sb("over", [P, E])
        over_before = sb("over_before", [P, E])
        far = sb("far", [P, TB, E])
        jump = sb("jump", [P, E])
        place = sb("place", [P, TB, E])
        tmpE = sb("tmpE", [P, TB, E])
        key = sb("key", [P, 2, TB])
        wgt = sb("wgt", [P, 2, TB])
        wtmp = sb("wtmp", [P, 2, TB])
        extra_f = sb("extra_f", [P, 4])
        extra = sb("extra", [P, 4], I32)

        psA = ctx.enter_context(nc.psum_tensor("psA", [P, 2, W], F32))
        psB = ctx.enter_context(nc.psum_tensor("psB", [P, 2, W], F32))
        psY = ctx.enter_context(nc.psum_tensor("psY", [P, 4, W], F32))

        x_in = [sem(f"x_in{tb}") for tb in range(TB)]
        gains_in = sem("gains_in")
        lam_in = sem("lam_in")
        gain_in = sem("gain_in")
        router_in = sem("router_in")
        slot_full = [sem(f"slot_full{r}") for r in range(RING)]
        hi_done = sem("hi_done")
        lo_dve = sem("lo_dve")
        lo_pool = sem("lo_pool")
        group_used = sem("group_used")
        consts = sem("consts")
        ones_set = sem("ones_set")
        gains_T = sem("gains_T")
        gains_set = sem("gains_set")
        lam_exp = sem("lam_exp")
        lam_dot = sem("lam_dot")
        ssq_done = sem("ssq_done")
        rstd_done = sem("rstd_done")
        rows_done = sem("rows_done")
        turn_done = sem("turn_done")
        xhi_done = sem("xhi_done")
        xlo_done = sem("xlo_done")
        qkv_done = sem("qkv_done")
        score_half = sem("score_half")
        score_done = sem("score_done")
        min_done = sem("min_done")
        exp_done = sem("exp_done")
        mixed = sem("mixed")
        probT_done = sem("probT_done")
        probT_out = sem("probT_out")
        pv_done = sem("pv_done")
        o_done = sem("o_done")
        o_ssq = sem("o_ssq")
        o_rstd = sem("o_rstd")
        res_done = sem("res_done")
        silu_done = sem("silu_done")
        hid_done = sem("hid_done")
        hidT_done = sem("hidT_done")
        hhi_done = sem("hhi_done")
        hlo_done = sem("hlo_done")
        chain_dve = sem("chain_dve")
        chain_pool = sem("chain_pool")
        chain_act = sem("chain_act")
        rt_split = sem("rt_split")
        logit_mm = sem("logit_mm")
        rowsplit = sem("rowsplit")
        wdiff = sem("wdiff")
        wexp = sem("wexp")
        member_set = sem("member_set")
        pos_mm = sem("pos_mm")
        table_set = sem("table_set")
        pick_set = sem("pick_set")
        gather_mm = sem("gather_mm")
        ihi_done = sem("ihi_done")
        ilo_done = sem("ilo_done")
        pickT_mm = sem("pickT_mm")
        pickT_set = sem("pickT_set")
        yhi_done = sem("yhi_done")
        ylo_done = sem("ylo_done")
        scatter_mm = sem("scatter_mm")
        add_done = sem("add_done")
        m_silu = sem("m_silu")
        m_hid = sem("m_hid")
        m_hidT = sem("m_hidT")
        m_hhi = sem("m_hhi")
        m_hlo = sem("m_hlo")
        out_rows = sem("out_rows")
        stored = sem("stored")

        block = ctx.enter_context(nc.Block())

        def repeat(ap, dim, n):
            layout = [list(d) for d in ap.ap]
            return bass.AP(ap.tensor, ap.offset, layout[:dim] + [[0, n]] + layout[dim:])

        def f(ap):
            return ap.bitcast(F32)

        def ring_group(s, g):
            return ring[:, s % RING, g * GROUP:(g + 1) * GROUP]

        def wait_group(eng, n):
            if by_pool[n]:
                eng.wait_ge(lo_pool, pool_upto[n + 1])
            else:
                eng.wait_ge(lo_dve, dve_upto[n + 1])

        def n_items(eng):
            eng.wait_ge(table_set, 1)
            return eng.value_load(extra[0:1, 0:1], min_val=0, max_val=3) + E

        def slot_landed(i, j):
            r = (NS + j) % RING
            dense = sum(1 for s in range(NS) if s % RING == r)
            return i * (16 * IS // RING) + 16 * (dense + j // RING + 1)

        def used_at(i, m):
            return i * IG + (NG + m)

        def wait_item_group(eng, i, m):
            pool_m, rest = divmod(m, POOL_EVERY)
            if rest == POOL_EVERY - 1:
                eng.wait_ge(lo_pool, i * (IG // POOL_EVERY) + (pool_upto[NG] + pool_m + 1))
            else:
                eng.wait_ge(lo_dve, i * (IG - IG // POOL_EVERY) + (dve_upto[NG] + m - pool_m + 1))

        BUILDS = [("norm", 0), ("attn", 0), ("norm", 1), ("norm", 2), ("attn", 1), ("norm", 3)]
        ROWS_BEFORE = [0, 2, 4, 6, None, 8]
        GAIN_ROW = (0, 2 * KD, KD, 3 * KD)
        ROWS_GAINED = 11

        def turned(b, q):
            if BUILDS[b][0] == "norm":
                return psY[:, q, :]
            return psA[:, q, :] if q < 2 else psY[:, q - 2, :]

        @block.sync
        def _(sp):
            for tb in range(TB):
                sp.dma_start(res[:, tb, :], x[0, tb * P:(tb + 1) * P, :]).then_inc(x_in[tb], 16)
            sp.dma_start(gain_rows[0:2 * KD, :], norm_mix.rearrange("l (k p) -> (l k) p", p=P)).then_inc(gains_in, 16)
            sp.dma_start(gain_rows[2 * KD:4 * KD, :], norm_ffn.rearrange("l (k p) -> (l k) p", p=P)).then_inc(gains_in, 16)
            sp.dma_start(gain_rows[4 * KD:4 * KD + 1, :], diff_subln[:, :]).then_inc(gains_in, 16)

            for s, (src, groups) in enumerate(slots):
                if s == 2:
                    sp.dma_start(lam, diff_lambda[0].partition_broadcast(P)).then_inc(lam_in, 16)
                    sp.dma_start(rt[:, :, :], moe_router[0].rearrange("(k p) e -> p k e", p=P)).then_inc(router_in, 16)
                if s >= RING:
                    n = first_group[s - RING + 1]
                    sp.wait_ge(lo_dve, dve_upto[n])
                    sp.wait_ge(lo_pool, pool_upto[n])
                dst = ring[:, s % RING, 0:groups * GROUP].rearrange("p (k n) -> p k n", n=src.shape[2])
                sp.dma_start(dst, src).then_inc(slot_full[s % RING], 16)

            dve_past = sp.alloc_register("dve_past")
            pool_past = sp.alloc_register("pool_past")
            sp.reg_mov(dve_past, dve_upto[NG] + (GS - POOL_GS) * (1 - RING))
            sp.reg_mov(pool_past, pool_upto[NG] + POOL_GS * (1 - RING))

            def load(r, dst, src):
                sp.wait_ge(lo_dve, dve_past)
                sp.wait_ge(lo_pool, pool_past)
                sp.dma_start(dst, src).then_inc(slot_full[r], 16)
                sp.reg_add(dve_past, dve_past, GS - POOL_GS)
                sp.reg_add(pool_past, pool_past, POOL_GS)

            def item(e):
                for j, (kind, c) in enumerate(item_slots):
                    r = (NS + j) % RING
                    if kind == "down":
                        src = moe_w_down[0][e, c * W:(c + 1) * W, :].rearrange("(g p) n -> p g n", p=P)
                    else:
                        w = moe_w_gate if kind == "gate" else moe_w_up
                        src = w[0][e, :, c * W:(c + 1) * W].rearrange("(k p) n -> p k n", p=P)
                    load(r, ring[:, r, :].rearrange("p (k n) -> p k n", n=src.shape[2]), src)

            with sp.Fori(0, E) as i:
                item(i)
            n = n_items(sp)
            with sp.If(n > E):
                with sp.Fori(E, n) as i:
                    e = sp.value_load(extra[0:1, bass.ds(i - (E - 1), 1)], min_val=0, max_val=E - 1)
                    item(e)
            r = NS % RING
            load(r, ring[:, r, 0:2], moe_w_down[0][0, 0:P, 0:2])
            for tb in range(TB):
                sp.wait_ge(out_rows, tb + 1)
                sp.dma_start(out[0, tb * P:(tb + 1) * P, :], rowbuf[:, tb, :]).then_inc(stored, 16)
            sp.wait_ge(stored, 16 * TB)

        @block.scalar
        def _(act):
            split = [0]

            def split_to(n):
                for m in range(split[0], min(n, NG)):
                    s, g = group_of[m]
                    if g == 0:
                        act.wait_ge(slot_full[s % RING], 16 * (s // RING + 1))
                    if m >= HL:
                        act.wait_ge(group_used, m - HL + 1)
                    nc.scalar.copy(whi[:, m % HL, :], ring_group(s, g)).then_inc(hi_done, 1)
                split[0] = max(split[0], min(n, NG))

            def square_sums(norm, arrived):
                for tb in range(TB):
                    act.wait_ge(*arrived(tb))
                    nc.scalar.activation(rowbuf[:, tb, :], res[:, tb, :], ACT.Square,
                                         accum_out=ssq[:, norm, tb:tb + 1]).then_inc(ssq_done, 1)

            def build(b, first=0, last=KD // 2):
                kind, j = BUILDS[b]
                for q in range(first, last):
                    bank = turned(b, q)
                    act.wait_ge(turn_done, 4 * b + q + 1)
                    if kind == "norm":
                        for k in range(2 * q, 2 * q + 2):
                            col = GAIN_ROW[j] + k
                            ins = nc.scalar.activation(xhi[:, k, :], bank[:, (k % 2) * T:(k % 2 + 1) * T], ACT.Copy,
                                                       scale=gain_cols[:, col:col + 1])
                    elif j == 0:
                        ins = nc.scalar.activation(xhi[:, 2 * q:2 * q + 2, :], bank, ACT.Copy,
                                                   scale=gain_cols[:, 4 * KD:4 * KD + 1])
                    else:
                        ins = nc.scalar.copy(xhi[:, 2 * q:2 * q + 2, :], bank)
                    ins.then_inc(xhi_done, 1)

            def exps(layer, u):
                n = UNITS * layer + u
                keys = (u % TB + 1) * P
                if u >= 2:
                    act.wait_ge(probT_done, n - 1)
                act.wait_ge(min_done, n + 1)
                for i in range(2):
                    ins = nc.scalar.activation(probs[:, u % 2, i, 0:keys], psY[:, u % 2, i * T:i * T + keys], ACT.Exp,
                                               scale=-1.0, bias=score_min[:, layer, u, i:i + 1],
                                               accum_out=prob_sum[:, layer, u, i:i + 1])
                ins.then_inc(exp_done, 1)

            def copy_probT(layer, u):
                n = UNITS * layer + u
                blocks = (u % TB + 1) * (1 if layer == 0 else 2)
                act.wait_ge(probT_done, n + 1)
                if u >= 2:
                    act.wait_ge(pv_done, n - 1)
                nc.scalar.copy(probsT[:, u % 2, 0:blocks, :], psY[:, 2, 0:blocks * P]).then_inc(probT_out, 1)

            def head_square(u):
                pair, tb = u // TB, u % TB
                at = tb * (PAIRS // 2) + pair % (PAIRS // 2)
                act.wait_ge(o_done, u + 1)
                if u >= 1:
                    act.wait_ge(o_ssq, u)
                nc.scalar.activation(junk[:, :], rowbuf[:, tb, pair * P:(pair + 1) * P], ACT.Square,
                                     accum_out=head_ssq[:, pair // (PAIRS // 2), at:at + 1]).then_inc(o_ssq, 1)

            def copy_out(layer, j):
                half, kind = divmod(j, 3)
                act.wait_ge(group_used, first_group[first_slot["qkv", layer] + j + 1])
                ps = psA if j % 2 == 0 else psB
                if kind == 0:
                    for b in range(4):
                        pair = 4 * half + b
                        ins = nc.scalar.activation(qT[:, pair, :], ps[:, b // 2, (b % 2) * T:(b % 2 + 1) * T],
                                                   ACT.Copy, scale=q_scale[:, layer, pair:pair + 1])
                elif kind == 1:
                    ins = nc.scalar.copy(kT[:, 4 * half:4 * half + 4, :], ps[:, :, :])
                else:
                    ins = nc.scalar.copy(val[:, :, half * W:(half + 1) * W], ps[:, :, :])
                ins.then_inc(qkv_done, 1)

            square_sums(0, lambda tb: (x_in[tb], 16))
            split_to(HL)
            act.wait_ge(gains_set, 1)
            for layer in range(2):
                if layer == 1:
                    square_sums(2, lambda tb: (res_done, TB + tb + 1))
                build(3 * layer)
                s0 = first_slot["qkv", layer]
                for j in range(2):
                    split_to(first_group[s0 + j + 1] + AHEAD)
                    copy_out(layer, j)
                if layer == 0:
                    act.wait_ge(lam_dot, 1)
                    nc.scalar.activation(small[:, 2:4], small[:, 0:2], ACT.Exp).then_inc(lam_exp, 1)
                for t in range(STEPS):
                    if layer == 0 and t >= 3:
                        head_square(t - 3)
                    if t < UNITS:
                        exps(layer, t)
                    if t == HALF_BUILD:
                        build(3 * layer + 1, 0, 2)
                    split_to(filled[layer][t] + AHEAD + FILL[layer][t] // 2)
                    if 1 <= t <= UNITS:
                        copy_probT(layer, t - 1)
                    split_to(filled[layer][t + 1] + AHEAD)
                    for s in ends[layer][t]:
                        copy_out(layer, s - s0)
                if layer == 0:
                    head_square(UNITS - 1)
                split_to(first_group[first_slot["wo", layer] + 1] + AHEAD)
                build(3 * layer + 1, 2, 4)
                if layer == 1:
                    act.dma_start(gain, norm_ffn[1].partition_broadcast(P)).then_inc(gain_in, 16)
                split_to(first_group[first_slot["wo", layer] + 2] + HL)
                square_sums(2 * layer + 1, lambda tb: (res_done, 2 * TB * layer + tb + 1))
                if layer == 0:
                    build(2)
                    for c in range(NF):
                        w = width[c]
                        split_to(first_group[gate_slot[c] + 1] + AHEAD)
                        act.wait_ge(group_used, first_group[gate_slot[c] + 1])
                        nc.scalar.activation(hid[:, :, 0:w], psA[:, :, 0:w], ACT.Silu).then_inc(silu_done, 1)
                        last = down_slot[c - 1] if c else up_slot[c]
                        split_to(first_group[last + 1] + AHEAD)
                        for q in range(w // (2 * P)):
                            act.wait_ge(hidT_done, 2 * c + q + 1)
                            nc.scalar.copy(hhi[:, 2 * q:2 * q + 2, :], psB[:, q, :]).then_inc(hhi_done, 1)
                    split_to(first_group[first_slot["qkv", 1]] + HL)

            act.wait_ge(router_in, 16)
            nc.scalar.copy(rt_hi[:, :, :], rt[:, :, :]).then_inc(rt_split, 1)
            build(5)
            act.wait_ge(wdiff, 1)
            nc.scalar.activation(wtmp[:, 0, :], wtmp[:, 1, :], ACT.Exp).then_inc(wexp, 1)
            act.wait_ge(rows_done, ROWS_GAINED)
            act.wait_ge(logit_mm, 1)
            nc.scalar.copy(xhi[:, :, :].rearrange("p k t -> p (k t)"),
                           rowbuf[:, :, :].rearrange("p b d -> p (b d)")).then_inc(rowsplit, 1)

            def item_split(i, first, last):
                for m in range(first, last):
                    j, g = m // GS, m % GS
                    r = (NS + j) % RING
                    if g == 0:
                        act.wait_ge(slot_full[r], slot_landed(i, j))
                    act.wait_ge(group_used, used_at(i, m - HL + 1))
                    nc.scalar.copy(whi[:, (NG + m) % HL, :], ring[:, r, g * GROUP:(g + 1) * GROUP]).then_inc(hi_done, 1)

            def gather_hi(i):
                for q in range(2):
                    act.wait_ge(gather_mm, 2 * i + (q + 1))
                    nc.scalar.copy(ihi[:, 4 * q:4 * q + 4, :], psY[:, 2 + q, :]).then_inc(ihi_done, 1)

            def hidden_hi(i, c):
                act.wait_ge(m_hidT, i * NE + (c + 1))
                nc.scalar.copy(hhi[:, :, 0:P], psB[:, 1, :].rearrange("p (b t) -> p b t", t=P)).then_inc(m_hhi, 1)

            n = n_items(act)
            item_split(0, 0, AHEAD)
            gather_hi(0)
            with act.Fori(0, n) as i:
                done = AHEAD
                for c in range(NE):
                    stop = GS * (item_slot["gate", c] + 1) + AHEAD
                    item_split(i, done, stop)
                    done = stop
                    if c:
                        hidden_hi(i, c - 1)
                    act.wait_ge(group_used, used_at(i, stop - AHEAD))
                    nc.scalar.activation(hid[:, 0, :], psA[:, 0, :], ACT.Silu).then_inc(m_silu, 1)
                stop = GS * item_slot["down", NE - 1] + AHEAD
                item_split(i, done, stop)
                hidden_hi(i, NE - 1)
                gather_hi(i + 1)
                item_split(i, stop, IG)
                item_split(i + 1, 0, AHEAD)
                act.wait_ge(group_used, used_at(i, IG))
                act.wait_ge(pickT_set, 2 * i + 2)
                nc.scalar.activation(yhi[:, :], psY[:, 0:2, :].rearrange("p b n -> p (b n)"), ACT.Copy,
                                     scale=gate_of_slot[:, 0:1]).then_inc(yhi_done, 1)
            act.dma_start(gain, final_norm.partition_broadcast(P)).then_inc(gain_in, 16)
            square_sums(4, lambda tb: (add_done, n * TB + (tb + 1)))

        @block.gpsimd
        def _(pool):
            links = [0]

            def link(ins):
                links[0] += 1
                ins.then_inc(chain_pool, 1)
                pool.wait_ge(chain_pool, links[0])

            def select(ap, fill, op, base, pattern, per_row):
                return nc.gpsimd.affine_select(out=ap, in_=ap, compare_op=op, fill=fill, base=base,
                                               pattern=pattern, channel_multiplier=per_row)

            nc.gpsimd.memset(halfneg[:, :], -0.5)
            link(nc.gpsimd.memset(ident[:, :], 0.0))
            link(select(ident[:, :], 1.0, ALU.not_equal, 0, [[-1, P]], 1))
            nc.gpsimd.memset(ones[:, :], 1.0)
            link(nc.gpsimd.memset(before[:, :], 1.0))
            link(select(before[:, :], 0.0, ALU.is_gt, 0, [[1, P]], -1))
            nc.gpsimd.iota(slotno[:, :], pattern=[[1, P]], base=0, channel_multiplier=0,
                           allow_small_or_imprecise_dtypes=True)
            nc.gpsimd.iota(expert_no[:, :], pattern=[[1, E]], base=0, channel_multiplier=0,
                           allow_small_or_imprecise_dtypes=True)
            nc.gpsimd.iota(dist[:, 0:P], pattern=[[-1, P]], base=0, channel_multiplier=1,
                           allow_small_or_imprecise_dtypes=True)
            link(nc.gpsimd.iota(dist[:, P:3 * P], pattern=[[-1, T]], base=P, channel_multiplier=1,
                                allow_small_or_imprecise_dtypes=True))
            link(select(dist[:, 0:P], BIG, ALU.is_ge, 0, [[-1, P]], 1))
            select(dist[:, P:3 * P], BIG, ALU.is_ge, P, [[-1, T]], 1).then_inc(consts, 1)

            halved = [0]

            def halve_to(n):
                for m in range(halved[0], min(n, NG)):
                    if by_pool[m]:
                        s, g = group_of[m]
                        pool.wait_ge(hi_done, m + 1)
                        nc.gpsimd.tensor_tensor(wlo[:, m % HL, :], ring_group(s, g), f(whi[:, m % HL, :]),
                                                ALU.subtract).then_inc(lo_pool, 1)
                halved[0] = max(halved[0], min(n, NG))

            def root(norm):
                for tb in range(TB):
                    pool.wait_ge(ssq_done, TB * norm + tb + 1)
                    at = rstd[:, norm, tb:tb + 1]
                    link(nc.gpsimd.tensor_scalar(at, ssq[:, norm, tb:tb + 1], 1.0 / D, EPS, ALU.mult, ALU.add))
                    nc.gpsimd.tensor_tensor(at, at, halfneg[:, 0:1], ALU.pow).then_inc(rstd_done, 1)

            root(0)
            for half in range(2):
                if half == 0:
                    halve_to(filled[0][UNITS // 2 + 2] + AHEAD)
                else:
                    halve_to(first_group[first_slot["wo", 0] + 1] + AHEAD)
                pool.wait_ge(o_ssq, (half + 1) * UNITS // 2)
                at = head_rstd[:, half, :]
                link(nc.gpsimd.tensor_scalar(at, head_ssq[:, half, :], 1.0 / P, SUB_EPS, ALU.mult, ALU.add))
                nc.gpsimd.tensor_tensor(at, at, halfneg[:, 0:PAIRS], ALU.pow).then_inc(o_rstd, 1)
            halve_to(first_group[first_slot["ffn", 0]] + HL)
            root(1)
            halve_to(first_group[first_slot["qkv", 1]] + HL)
            root(2)
            halve_to(NG)
            root(3)
            nc.gpsimd.memset(f(pickT[:, :]), 0.0)
            nc.gpsimd.memset(f(yhi[:, :]), 0.0)
            nc.gpsimd.memset(f(ylo[:, :]), 0.0).then_inc(ylo_done, 1)
            n = n_items(pool)
            with pool.Fori(0, n) as i:
                for m in range(POOL_EVERY - 1, IG, POOL_EVERY):
                    j, g = m // GS, m % GS
                    pool.wait_ge(hi_done, used_at(i, m + 1))
                    nc.gpsimd.tensor_tensor(wlo[:, (NG + m) % HL, :], ring[:, (NS + j) % RING, g * GROUP:(g + 1) * GROUP],
                                            f(whi[:, (NG + m) % HL, :]), ALU.subtract).then_inc(lo_pool, 1)
            root(4)

        @block.vector
        def _(dve):
            links = [0]

            def link(ins):
                links[0] += 1
                ins.then_inc(chain_dve, 1)
                dve.wait_ge(chain_dve, links[0])

            halved = [0]

            def halve_to(n):
                for m in range(halved[0], min(n, NG)):
                    if not by_pool[m]:
                        s, g = group_of[m]
                        dve.wait_ge(hi_done, m + 1)
                        nc.vector.tensor_tensor(wlo[:, m % HL, :], ring_group(s, g), f(whi[:, m % HL, :]),
                                                ALU.subtract).then_inc(lo_dve, 1)
                halved[0] = max(halved[0], min(n, NG))

            def norm_diag(norm):
                for tb in range(TB):
                    dve.wait_ge(rstd_done, TB * norm + tb + 1)
                    nc.vector.tensor_scalar(rowbuf[:, tb, 0:P], ident[:, :], rstd[:, norm, tb:tb + 1], None,
                                            ALU.mult).then_inc(rows_done, 1)

            def build(b, first=0, last=KD // 2):
                kind, j = BUILDS[b]
                for q in range(first, last):
                    bank = turned(b, q)
                    dve.wait_ge(xhi_done, 4 * b + q + 1)
                    if kind == "norm":
                        for k in range(2 * q, 2 * q + 2):
                            col = GAIN_ROW[j] + k
                            ins = nc.vector.scalar_tensor_tensor(
                                out=xlo[:, k, :], in0=bank[:, (k % 2) * T:(k % 2 + 1) * T],
                                scalar=gain_cols[:, col:col + 1], in1=f(xhi[:, k, :]), op0=ALU.mult, op1=ALU.subtract)
                    else:
                        hi = f(xhi[:, 2 * q:2 * q + 2, :]).rearrange("p k t -> p (k t)")
                        lo = xlo[:, 2 * q:2 * q + 2, :].rearrange("p k t -> p (k t)")
                        if j == 0:
                            ins = nc.vector.scalar_tensor_tensor(
                                out=lo, in0=bank, scalar=gain_cols[:, 4 * KD:4 * KD + 1], in1=hi,
                                op0=ALU.mult, op1=ALU.subtract)
                        else:
                            ins = nc.vector.tensor_tensor(lo, bank, hi, ALU.subtract)
                    ins.then_inc(xlo_done, 1)

            def minima(layer, u):
                n = UNITS * layer + u
                keys = (u % TB + 1) * P
                d = dist[:, 0:P] if u % TB == 0 else dist[:, P:3 * P]
                dve.wait_ge(score_done, n + 1)
                for i in range(2):
                    s = psY[:, u % 2, i * T:i * T + keys]
                    ins = nc.vector.tensor_tensor_reduce(
                        out=s, in0=s, in1=d, scale=slopes[layer][2 * (u // TB) + i], scalar=3e38, op0=ALU.add,
                        op1=ALU.min, accum_out=score_min[:, layer, u, i:i + 1])
                ins.then_inc(min_done, 1)

            def combine(u):
                keys = (u % TB + 1) * P
                dve.wait_ge(exp_done, u + 1)
                link(nc.vector.reciprocal(prob_inv[:, 0, u, :], prob_sum[:, 0, u, :]))
                link(nc.vector.tensor_scalar(mix[:, u:u + 1], prob_sum[:, 0, u, 0:1], prob_inv[:, 0, u, 1:2],
                                             small[:, 4:5], ALU.mult, ALU.mult))
                nc.vector.scalar_tensor_tensor(
                    out=probs[:, u % 2, 0, 0:keys], in0=probs[:, u % 2, 1, 0:keys], scalar=mix[:, u:u + 1],
                    in1=probs[:, u % 2, 0, 0:keys], op0=ALU.mult, op1=ALU.add).then_inc(mixed, 1)

            def invert(u):
                dve.wait_ge(exp_done, UNITS + u + 1)
                nc.vector.reciprocal(prob_inv[:, 1, u, :], prob_sum[:, 1, u, :]).then_inc(mixed, 1)

            def output_rows(layer, u):
                pair, tb = u // TB, u % TB
                dve.wait_ge(pv_done, UNITS * layer + u + 1)
                rows_ = rowbuf[:, tb, pair * P:(pair + 1) * P]
                if layer == 0:
                    nc.vector.tensor_scalar(rows_, psY[:, 3, 0:P], prob_inv[:, 0, u, 0:1], None,
                                            ALU.mult).then_inc(o_done, 1)
                else:
                    dve.wait_ge(mixed, UNITS + u + 1)
                    nc.vector.tensor_tensor(rows_.rearrange("p (i d) -> p i d", i=2),
                                            psY[:, 3, 0:P].rearrange("p (i d) -> p i d", i=2),
                                            repeat(prob_inv[:, 1, u, :], 2, 64), ALU.mult).then_inc(o_done, 1)

            def norm_heads(half):
                dve.wait_ge(o_rstd, half + 1)
                for tb in range(TB):
                    rows_ = rowbuf[:, tb, half * W:(half + 1) * W].rearrange("p (h d) -> p h d", d=P)
                    factor = head_rstd[:, half, tb * (PAIRS // 2):(tb + 1) * (PAIRS // 2)]
                    ins = nc.vector.tensor_tensor(rows_, rows_, repeat(factor, 2, P), ALU.mult)
                ins.then_inc(rows_done, 1)

            def add_to_residual(tb, ps):
                r = res[:, tb, :]
                return nc.vector.tensor_tensor(r, ps.rearrange("p b n -> p (b n)"), r, ALU.add)

            for layer in range(2):
                for pair in range(PAIRS):
                    for i in range(2):
                        nc.vector.memset(q_scale[64 * i:64 * i + 64, layer, pair:pair + 1],
                                         -SCALE / slopes[layer][2 * pair + i])
            halve_to(HL)
            dve.wait_ge(consts, 1)
            norm_diag(0)
            dve.wait_ge(gains_T, 1)
            nc.vector.tensor_copy(gain_cols[:, 0:4 * KD], psA[:, 0, 0:4 * KD])
            nc.vector.tensor_scalar(gain_cols[:, 4 * KD:4 * KD + 1], psA[:, 0, 4 * KD:4 * KD + 1], SUB, None,
                                    ALU.mult).then_inc(gains_set, 1)
            for layer in range(2):
                build(3 * layer)
                halve_to(filled[layer][0] + AHEAD)
                if layer == 0:
                    dve.wait_ge(lam_in, 16)
                    for i in range(2):
                        ins = nc.vector.tensor_tensor_reduce(
                            out=lam_prod, in0=lam[:, 2 * i, :], in1=lam[:, 2 * i + 1, :], scale=1.0, scalar=0.0,
                            op0=ALU.mult, op1=ALU.add, accum_out=small[:, i:i + 1])
                        if i == 0:
                            link(ins)
                    ins.then_inc(lam_dot, 1)
                    dve.wait_ge(lam_exp, 1)
                    link(nc.vector.tensor_tensor(small[:, 5:6], small[:, 3:4], small[:, 2:3], ALU.subtract))
                    link(nc.vector.tensor_scalar(small[:, 4:5], small[:, 5:6], -LAM_INIT, None, ALU.add))
                for t in range(STEPS):
                    if 1 <= t <= UNITS:
                        if layer == 0:
                            combine(t - 1)
                        else:
                            invert(t - 1)
                    if t < UNITS:
                        minima(layer, t)
                    if layer == 0 and t == HALF_BUILD - 1:
                        norm_heads(0)
                    if t == HALF_BUILD:
                        build(3 * layer + 1, 0, 2)
                    halve_to(filled[layer][t] + AHEAD + FILL[layer][t] // 2)
                    if t >= 2:
                        output_rows(layer, t - 2)
                    halve_to(filled[layer][t + 1] + AHEAD)
                if layer == 0:
                    norm_heads(1)
                halve_to(first_group[first_slot["wo", layer] + 1] + AHEAD)
                build(3 * layer + 1, 2, 4)
                end = first_group[first_slot["wo", layer] + 2]
                halve_to(end + HL)
                dve.wait_ge(group_used, end)
                for tb, ps in enumerate((psA, psB)):
                    add_to_residual(tb, ps[:, :, :]).then_inc(res_done, 1)
                if layer == 1:
                    break
                norm_diag(1)
                build(2)
                for c in range(NF):
                    w = width[c]
                    halve_to(first_group[up_slot[c] + 1] + AHEAD)
                    dve.wait_ge(silu_done, c + 1)
                    dve.wait_ge(group_used, first_group[up_slot[c] + 1])
                    nc.vector.tensor_tensor(hid[:, :, 0:w], psB[:, :, 0:w], hid[:, :, 0:w], ALU.mult).then_inc(hid_done, 1)
                    last = down_slot[c - 1] if c else up_slot[c]
                    halve_to(first_group[last + 1] + AHEAD)
                    for q in range(w // (2 * P)):
                        dve.wait_ge(hhi_done, 2 * c + q + 1)
                        nc.vector.tensor_tensor(
                            hlo[:, 2 * q:2 * q + 2, :].rearrange("p k t -> p (k t)"), psB[:, q, :],
                            f(hhi[:, 2 * q:2 * q + 2, :]).rearrange("p k t -> p (k t)"), ALU.subtract).then_inc(hlo_done, 1)
                end = first_group[first_slot["qkv", 1]]
                halve_to(end + HL)
                dve.wait_ge(group_used, end)
                for tb in range(TB):
                    add_to_residual(tb, psY[:, 2 * tb:2 * tb + 2, :]).then_inc(res_done, 1)
                norm_diag(2)

            dve.wait_ge(rt_split, 1)
            nc.vector.tensor_tensor(rt_lo[:, :, :], rt[:, :, :], f(rt_hi[:, :, :]), ALU.subtract).then_inc(rt_split, 1)
            norm_diag(3)
            build(5)
            dve.wait_ge(gain_in, 16)
            dve.wait_ge(turn_done, 4 * 6)
            for tb in range(TB):
                ins = nc.vector.scalar_tensor_tensor(out=rowbuf[:, tb, :], in0=res[:, tb, :], scalar=rstd[:, 3, tb:tb + 1],
                                                     in1=gain, op0=ALU.mult, op1=ALU.mult)
            ins.then_inc(rows_done, 1)
            dve.wait_ge(logit_mm, 1)
            link(nc.vector.tensor_copy(logit[:, :, :], psA[:, 0, 0:TB * E].rearrange("p (b e) -> p b e", e=E)))
            for tb in range(TB):
                link(nc.vector.max(top[:, tb, :], logit[:, tb, :]))
            for tb in range(TB):
                link(nc.vector.max_index(top_at[:, tb, :], top[:, tb, :], logit[:, tb, :]))
            nc.vector.tensor_tensor(wtmp[:, 1, :], top[:, :, 1], top[:, :, 0], ALU.subtract).then_inc(wdiff, 1)
            link(nc.vector.tensor_copy(top_atf[:, :, :], top_at[:, :, :]))
            for tb in range(TB):
                nc.vector.tensor_scalar(isA[:, tb, :], expert_no[:, :], top_atf[:, tb, 0:1], None, ALU.is_equal)
                ins = nc.vector.tensor_scalar(isB[:, tb, :], expert_no[:, :], top_atf[:, tb, 1:2], None, ALU.is_equal)
            link(ins)
            nc.vector.tensor_tensor(member[:, :, :], isA[:, :, :], isB[:, :, :], ALU.add).then_inc(member_set, 1)
            dve.wait_ge(wexp, 1)
            link(nc.vector.tensor_scalar(wtmp[:, 1, :], wtmp[:, 0, :], 1.0, None, ALU.add))
            link(nc.vector.reciprocal(wgt[:, 0, :], wtmp[:, 1, :]))
            link(nc.vector.tensor_tensor(wgt[:, 1, :], wgt[:, 0, :], wtmp[:, 0, :], ALU.mult))
            dve.wait_ge(pos_mm, 1)
            link(nc.vector.tensor_copy(pos[:, :, :], psA[:, 1, 0:3 * E].rearrange("p (b e) -> p b e", e=E)))
            link(nc.vector.tensor_scalar(over[:, :], pos[:, 2, :], float(P), None, ALU.is_gt))
            link(nc.vector.memset(over_before[:, :], 0.0))
            for e in range(1, E):
                link(nc.vector.tensor_tensor(over_before[:, e:e + 1], over_before[:, e - 1:e], over[:, e - 1:e], ALU.add))
            link(nc.vector.tensor_tensor(extra_f[:, 0:1], over_before[:, E - 1:E], over[:, E - 1:E], ALU.add))
            for k in range(3):
                link(nc.vector.tensor_scalar(far[:, 0, :], over_before[:, :], float(k), None, ALU.is_equal))
                link(nc.vector.tensor_tensor(far[:, 0, :], far[:, 0, :], over[:, :], ALU.mult))
                link(nc.vector.tensor_tensor_reduce(
                    out=far[:, 1, :], in0=far[:, 0, :], in1=expert_no[:, :], scale=1.0, scalar=0.0, op0=ALU.mult,
                    op1=ALU.add, accum_out=extra_f[:, k + 1:k + 2]))
            nc.vector.tensor_copy(extra[:, :], extra_f[:, :]).then_inc(table_set, 1)
            link(nc.vector.tensor_tensor(jump[:, :], over_before[:, :], expert_no[:, :], ALU.subtract))
            link(nc.vector.tensor_scalar(jump[:, :], jump[:, :], float(P), float(P * (E - 1)), ALU.mult, ALU.add))
            for tb in range(TB):
                link(nc.vector.tensor_scalar(far[:, tb, :], pos[:, tb, :], float(P), None, ALU.is_ge))
                link(nc.vector.tensor_tensor(far[:, tb, :], far[:, tb, :], jump[:, :], ALU.mult))
                link(nc.vector.scalar_tensor_tensor(out=place[:, tb, :], in0=expert_no[:, :], scalar=float(P),
                                                    in1=pos[:, tb, :], op0=ALU.mult, op1=ALU.add))
                link(nc.vector.tensor_tensor(place[:, tb, :], place[:, tb, :], far[:, tb, :], ALU.add))
                for a, chosen in enumerate((isA, isB)):
                    link(nc.vector.tensor_tensor_reduce(
                        out=tmpE[:, tb, :], in0=place[:, tb, :], in1=chosen[:, tb, :], scale=1.0, scalar=0.0,
                        op0=ALU.mult, op1=ALU.add, accum_out=key[:, a, tb:tb + 1]))
            dve.wait_ge(rowsplit, 1)
            nc.vector.tensor_tensor(xlo[:, :, :].rearrange("p k t -> p (k t)"), rowbuf[:, :, :].rearrange("p b d -> p (b d)"),
                                    f(xhi[:, :, :]).rearrange("p k t -> p (k t)"), ALU.subtract).then_inc(rowsplit, 1)

            def one_hots(i):
                for tb in range(TB):
                    ins = nc.vector.tensor_scalar(eqA[:, tb, :], slotno[:, :], key[:, 0, tb:tb + 1], None, ALU.is_equal)
                ins.then_inc(pick_set, 1)
                dve.wait_ge(pick_set, 4 * i + 1)
                for tb in range(TB):
                    ins = nc.vector.scalar_tensor_tensor(
                        out=pick[:, tb, :], in0=slotno[:, :], scalar=key[:, 1, tb:tb + 1], in1=eqA[:, tb, :],
                        op0=ALU.is_equal, op1=ALU.add)
                ins.then_inc(pick_set, 1)
                dve.wait_ge(pick_set, 4 * i + 2)
                for a, eq in enumerate((eqA, eqB)):
                    for tb in range(TB):
                        ins = nc.vector.tensor_scalar(eq[:, tb, :], slotno[:, :], key[:, a, tb:tb + 1], wgt[:, a, tb:tb + 1],
                                                      ALU.is_equal, ALU.mult)
                ins.then_inc(pick_set, 1)
                dve.wait_ge(pick_set, 4 * i + 3)
                nc.vector.tensor_scalar(key[:, :, :], key[:, :, :], -float(P), None, ALU.add).then_inc(pick_set, 1)
                dve.wait_ge(pick_set, 4 * i + 4)

            def item_halve(i, first, last):
                for m in range(first, last):
                    if m % POOL_EVERY != POOL_EVERY - 1:
                        dve.wait_ge(hi_done, used_at(i, m + 1))
                        g = m % GS
                        nc.vector.tensor_tensor(
                            wlo[:, (NG + m) % HL, :], ring[:, (NS + m // GS) % RING, g * GROUP:(g + 1) * GROUP],
                            f(whi[:, (NG + m) % HL, :]), ALU.subtract).then_inc(lo_dve, 1)

            def gather_lo(i):
                for q in range(2):
                    dve.wait_ge(ihi_done, 2 * i + (q + 1))
                    nc.vector.tensor_tensor(
                        ilo[:, 4 * q:4 * q + 4, :].rearrange("p k t -> p (k t)"), psY[:, 2 + q, :],
                        f(ihi[:, 4 * q:4 * q + 4, :]).rearrange("p k t -> p (k t)"), ALU.subtract).then_inc(ilo_done, 1)

            def hidden_lo(i, c):
                dve.wait_ge(m_hhi, i * NE + (c + 1))
                nc.vector.tensor_tensor(hlo[:, :, 0:P], psB[:, 1, :].rearrange("p (b t) -> p b t", t=P),
                                        f(hhi[:, :, 0:P]), ALU.subtract).then_inc(m_hlo, 1)

            def add_scattered(i, tb):
                dve.wait_ge(scatter_mm, TB * i + (tb + 1))
                add_to_residual(tb, psY[:, 2:4, :]).then_inc(add_done, 1)

            one_hots(0)
            n = n_items(dve)
            item_halve(0, 0, AHEAD)
            gather_lo(0)
            with dve.Fori(0, n) as i:
                done = AHEAD
                for c in range(NE):
                    stop = GS * (item_slot["gate", c] + 1) + AHEAD
                    item_halve(i, done, stop)
                    if c == 0:
                        add_scattered(i, 0)
                    else:
                        hidden_lo(i, c - 1)
                    done, stop = stop, GS * (item_slot["up", c] + 1) + AHEAD
                    item_halve(i, done, stop)
                    done = stop
                    dve.wait_ge(m_silu, i * NE + (c + 1))
                    dve.wait_ge(group_used, used_at(i, stop - AHEAD))
                    nc.vector.tensor_tensor(hid[:, 0, :], psB[:, 0, :], hid[:, 0, :], ALU.mult).then_inc(m_hid, 1)
                    if c == 0:
                        add_scattered(i, 1)
                    if c == 1:
                        dve.wait_ge(pickT_mm, i + 1)
                        nc.vector.tensor_copy(pickT[:, :], psA[:, 1, 0:T]).then_inc(pickT_set, 1)
                        nc.vector.tensor_copy(gate_of_slot[:, :], psA[:, 1, T:T + 1]).then_inc(pickT_set, 1)
                        one_hots(i + 1)
                stop = GS * item_slot["down", NE - 1] + AHEAD
                item_halve(i, done, stop)
                hidden_lo(i, NE - 1)
                gather_lo(i + 1)
                item_halve(i, stop, IG)
                item_halve(i + 1, 0, AHEAD)
                dve.wait_ge(yhi_done, i + 1)
                nc.vector.scalar_tensor_tensor(out=ylo[:, :], in0=psY[:, 0:2, :].rearrange("p b n -> p (b n)"),
                                               scalar=gate_of_slot[:, 0:1], in1=f(yhi[:, :]), op0=ALU.mult,
                                               op1=ALU.subtract).then_inc(ylo_done, 1)
            for tb in range(TB):
                add_scattered(n, tb)
            dve.wait_ge(gain_in, 32)
            for tb in range(TB):
                dve.wait_ge(rstd_done, TB * 4 + tb + 1)
                nc.vector.scalar_tensor_tensor(out=rowbuf[:, tb, :], in0=res[:, tb, :], scalar=rstd[:, 4, tb:tb + 1],
                                               in1=gain, op0=ALU.mult, op1=ALU.mult).then_inc(out_rows, 1)

        @block.tensor
        def _(pe):
            mm = nc.tensor.matmul

            def three(ps, xh, xl, wh, wl, start, stop, shared=False):
                mm(ps, xh, wh, start=start, stop=False, skip_group_check=shared)
                mm(ps, xh, wl, start=False, stop=False, skip_group_check=shared)
                return mm(ps, xl, wh, start=False, stop=stop, skip_group_check=shared)

            def build(b, first=0, last=KD // 2):
                kind, j = BUILDS[b]
                for q in range(first, last):
                    if b == 4:
                        pe.wait_ge(o_done, UNITS + (q // 2 + 1) * UNITS // 2)
                    elif kind == "attn":
                        pe.wait_ge(rows_done, ROWS_BEFORE[b] + q // 2 + 1)
                    for tb in range(TB):
                        if kind == "norm" and q == 0:
                            pe.wait_ge(rows_done, ROWS_BEFORE[b] + tb + 1)
                        for k in range(2):
                            at = turned(b, q)[:, k * T + tb * P:k * T + (tb + 1) * P]
                            chunk = slice((2 * q + k) * P, (2 * q + k + 1) * P)
                            if kind == "norm":
                                ins = mm(at, res[:, tb, chunk], rowbuf[:, tb, 0:P], start=True, stop=True)
                            else:
                                ins = nc.tensor.transpose(at, rowbuf[:, tb, chunk], ident[:, :])
                    ins.then_inc(turn_done, 1)

            def cols_group(s, g, b, ps, w=W):
                n, per = first_group[s] + g, GROUP // w
                wait_group(pe, n)
                for kk in range(per):
                    k = per * g + kk
                    pe.wait_ge(xlo_done, 4 * b + k // 2 + 1)
                    for tb in range(TB):
                        xs = slice(tb * P, (tb + 1) * P)
                        ws = slice(kk * w, (kk + 1) * w)
                        ins = three(ps[:, tb, 0:w], xhi[:, k, xs], xlo[:, k, xs], whi[:, n % HL, ws],
                                    wlo[:, n % HL, ws], k == 0, k == KD - 1)
                ins.then_inc(group_used, 1)

            def cols_slot(s, b, ps, w=W):
                for g in range(slots[s][1]):
                    cols_group(s, g, b, ps, w)

            def turned_group(s, k, b, ps):
                n = first_group[s] + k
                wait_group(pe, n)
                pe.wait_ge(xlo_done, 4 * b + k // 2 + 1)
                for fb in range(4):
                    ws = slice(fb * P, (fb + 1) * P)
                    ins = three(ps[:, fb // 2, (fb % 2) * T:(fb % 2 + 1) * T], whi[:, n % HL, ws],
                                wlo[:, n % HL, ws], xhi[:, k, :], xlo[:, k, :],
                                k == 0 and fb % 2 == 0, k == KD - 1, shared=True)
                ins.then_inc(group_used, 1)

            def qkv_group(layer, j, g):
                if g == 0:
                    if j >= 2:
                        pe.wait_ge(qkv_done, 6 * layer + j - 1)
                    elif layer == 0:
                        pe.wait_ge(gains_set, 1)
                (cols_group if j % 3 == 2 else turned_group)(first_slot["qkv", layer] + j, g, 3 * layer,
                                                             psA if j % 2 == 0 else psB)

            def rows_group(s, g, left, outs, first, last):
                n, (k, half) = first_group[s] + g, divmod(g, 2)
                wait_group(pe, n)
                xh, xl = left(k)
                for tb in range(TB):
                    xs = slice(tb * P, (tb + 1) * P)
                    ins = three(outs[tb][:, half, :], xh[:, xs], xl[:, xs], whi[:, n % HL, :],
                                wlo[:, n % HL, :], first and k == 0, last and g >= slots[s][1] - 2)
                ins.then_inc(group_used, 1)

            def rows_slot(s, left, outs, first, last):
                for g in range(slots[s][1]):
                    rows_group(s, g, left, outs, first, last)

            def wo_group(layer, j, g):
                def attn_left(k):
                    if j == 0 and g == 0:
                        pe.wait_ge(xlo_done, 4 * (3 * layer + 1) + 2)
                    elif j == 1:
                        pe.wait_ge(xlo_done, 4 * (3 * layer + 1) + 2 + k // 2 + 1)
                    return xhi[:, 4 * j + k, :], xlo[:, 4 * j + k, :]
                rows_group(first_slot["wo", layer] + j, g, attn_left, (psA, psB), j == 0, j == 1)

            def fill(layer, first, last):
                for n in range(first, last):
                    s, g = group_of[n]
                    if s < first_slot["wo", layer]:
                        qkv_group(layer, s - first_slot["qkv", layer], g)
                    else:
                        wo_group(layer, s - first_slot["wo", layer], g)

            def scores(layer, u):
                n, pair, tb = UNITS * layer + u, u // TB, u % TB
                keys = (tb + 1) * P
                pe.wait_ge(qkv_done, 6 * layer + (2 if pair < PAIRS // 2 else 5))
                if u >= 2:
                    pe.wait_ge(exp_done, n - 1)
                for i in range(2):
                    rows_ = slice(64 * i, 64 * i + 64)
                    ins = mm(psY[:, u % 2, i * T:i * T + keys], qT[rows_, pair, tb * P:(tb + 1) * P],
                             kT[rows_, pair, 0:keys], start=True, stop=True)
                    if i == 0:
                        ins.then_inc(score_half, 1)
                        pe.wait_ge(score_half, n + 1)
                ins.then_inc(score_done, 1)

            def turn_probs(layer, u):
                n, tb = UNITS * layer + u, u % TB
                if layer == 0:
                    pe.wait_ge(mixed, u + 1)
                else:
                    pe.wait_ge(exp_done, n + 1)
                if u >= 1:
                    pe.wait_ge(probT_out, n)
                at = 0
                for i in range(1 if layer == 0 else 2):
                    for kb in range(tb + 1):
                        ins = nc.tensor.transpose(psY[:, 2, at * P:(at + 1) * P],
                                                  probs[:, u % 2, i, kb * P:(kb + 1) * P], ident[:, :])
                        at += 1
                ins.then_inc(probT_done, 1)

            def weigh_values(layer, u):
                n, pair, tb = UNITS * layer + u, u // TB, u % TB
                pe.wait_ge(probT_out, n + 1)
                pe.wait_ge(qkv_done, 6 * layer + (3 if pair < PAIRS // 2 else 6))
                if u >= 1:
                    pe.wait_ge(o_done, n)
                heads = 1 if layer == 0 else 2
                wide = P // heads
                for i in range(heads):
                    for kb in range(tb + 1):
                        c = pair * P + i * wide
                        ins = mm(psY[:, 3, i * wide:(i + 1) * wide], probsT[:, u % 2, i * (tb + 1) + kb, :],
                                 val[:, kb, c:c + wide], start=kb == 0, stop=kb == tb)
                ins.then_inc(pv_done, 1)

            pe.wait_ge(consts, 1)
            pe.wait_ge(gains_in, 16 * 3)
            nc.tensor.transpose(psA[:, 0, 0:4 * KD + 1], gain_rows[0:4 * KD + 1, :],
                                ident[0:4 * KD + 1, 0:4 * KD + 1]).then_inc(gains_T, 1)
            for layer in range(2):
                b = 3 * layer
                build(b)
                for j in range(2):
                    for g in range(GS):
                        qkv_group(layer, j, g)
                for t in range(STEPS):
                    start, stop = filled[layer][t], filled[layer][t + 1]
                    middle = stop - FILL[layer][t] // 2
                    if t < UNITS:
                        scores(layer, t)
                    if t == HALF_BUILD:
                        build(b + 1, 0, 2)
                    if t >= 2:
                        weigh_values(layer, t - 2)
                    fill(layer, start, middle)
                    if 1 <= t <= UNITS:
                        turn_probs(layer, t - 1)
                    fill(layer, middle, stop)
                fill(layer, filled[layer][STEPS], first_group[first_slot["wo", layer] + 1])
                build(b + 1, 2, 4)
                fill(layer, first_group[first_slot["wo", layer] + 1], first_group[first_slot["wo", layer] + 2])
                if layer == 1:
                    break
                build(2)
                for c in range(NF + 1):
                    if c < NF:
                        if c:
                            pe.wait_ge(silu_done, c)
                        cols_slot(gate_slot[c], 2, psA, width[c])
                        if c:
                            pe.wait_ge(hlo_done, 2 * c)
                        cols_slot(up_slot[c], 2, psB, width[c])
                    if c:
                        def hidden_left(g, c=c):
                            pe.wait_ge(hlo_done, 2 * (c - 1) + g // 2 + 1)
                            return hhi[:, g, :], hlo[:, g, :]
                        rows_slot(down_slot[c - 1], hidden_left, (psY[:, 0:2, :], psY[:, 2:4, :]), c == 1, c == NF)
                    if c < NF:
                        pe.wait_ge(hid_done, c + 1)
                        for q in range(width[c] // (2 * P)):
                            for fb in range(2):
                                for tb in range(TB):
                                    ins = nc.tensor.transpose(
                                        psB[:, q, fb * T + tb * P:fb * T + (tb + 1) * P],
                                        hid[:, tb, (2 * q + fb) * P:(2 * q + fb + 1) * P], ident[:, :])
                            ins.then_inc(hidT_done, 1)

            build(5)
            pe.wait_ge(rt_split, 2)
            for tb in range(TB):
                for k in range(KD):
                    pe.wait_ge(xlo_done, 4 * 5 + k // 2 + 1)
                    xs = slice(tb * P, (tb + 1) * P)
                    ins = three(psA[:, 0, tb * E:(tb + 1) * E], xhi[:, k, xs], xlo[:, k, xs], rt_hi[:, k, :],
                                rt_lo[:, k, :], k == 0, k == KD - 1)
            ins.then_inc(logit_mm, 1)
            pe.wait_ge(member_set, 1)
            mm(psA[:, 1, 0:E], before[:, :], member[:, 0, :], start=True, stop=True)
            mm(psA[:, 1, E:2 * E], before[:, :], member[:, 1, :], start=True, stop=False)
            mm(psA[:, 1, E:2 * E], ones[:, :], member[:, 0, :], start=False, stop=True)
            mm(psA[:, 1, 2 * E:3 * E], ones[:, :], member[:, 0, :], start=True, stop=False)
            mm(psA[:, 1, 2 * E:3 * E], ones[:, :], member[:, 1, :], start=False, stop=True).then_inc(pos_mm, 1)

            rows_hi = xhi[:, :, :].rearrange("p k t -> p (k t)")
            rows_lo = xlo[:, :, :].rearrange("p k t -> p (k t)")

            def gather(i):
                pe.wait_ge(pick_set, 4 * i + 2)
                for q in range(2):
                    for k in range(4 * q, 4 * q + 4):
                        for tb in range(TB):
                            for part, rows_ in enumerate((rows_hi, rows_lo)):
                                ins = mm(psY[:, 2 + q, (k % 4) * P:(k % 4 + 1) * P],
                                         rows_[:, tb * D + k * P:tb * D + (k + 1) * P], pick[:, tb, :],
                                         start=tb == 0 and part == 0, stop=tb == TB - 1 and part == 1)
                    ins.then_inc(gather_mm, 1)

            def scatter(i, tb):
                if tb == 0:
                    pe.wait_ge(ylo_done, i + 1)
                    pe.wait_ge(ilo_done, 2 * i + 2)
                else:
                    pe.wait_ge(add_done, TB * i + tb)
                for half in range(2):
                    ws = slice(half * W, (half + 1) * W)
                    mm(psY[:, 2 + half, :], pickT[:, tb * P:(tb + 1) * P], yhi[:, ws], start=True, stop=False)
                    ins = mm(psY[:, 2 + half, :], pickT[:, tb * P:(tb + 1) * P], ylo[:, ws], start=False, stop=True)
                ins.then_inc(scatter_mm, 1)

            def hidden_turn(i, c):
                pe.wait_ge(m_hid, i * NE + (c + 1))
                for fb in range(FBW):
                    ins = nc.tensor.transpose(psB[:, 1, fb * P:(fb + 1) * P], hid[:, 0, fb * P:(fb + 1) * P], ident[:, :])
                ins.then_inc(m_hidT, 1)

            def item_slot_products(i, j):
                kind, c = item_slots[j]
                if kind == "gate" and c:
                    pe.wait_ge(m_silu, i * NE + c)
                if kind == "down":
                    pe.wait_ge(m_hlo, i * NE + (c + 1))
                for g in range(GS):
                    m = GS * j + g
                    at = (NG + m) % HL
                    wait_item_group(pe, i, m)
                    if kind == "down":
                        k, half = divmod(g, 2)
                        ins = three(psY[:, half, :], hhi[:, k, 0:P], hlo[:, k, 0:P], whi[:, at, :], wlo[:, at, :],
                                    c == 0 and k == 0, c == NE - 1 and k == FBW - 1)
                    else:
                        ps = (psA if kind == "gate" else psB)[:, 0, :]
                        ins = three(ps, ihi[:, g, :], ilo[:, g, :], whi[:, at, :], wlo[:, at, :], g == 0, g == KD - 1)
                    ins.then_inc(group_used, 1)

            pe.wait_ge(rowsplit, 2)
            gather(0)
            n = n_items(pe)
            with pe.Fori(0, n) as i:
                pe.wait_ge(ilo_done, 2 * i + 2)
                for j, (kind, c) in enumerate(item_slots):
                    if j == IS - 1:
                        hidden_turn(i, NE - 1)
                        gather(i + 1)
                    item_slot_products(i, j)
                    if kind == "gate" and c == 0:
                        scatter(i, 0)
                    if kind == "up" and c == 0:
                        scatter(i, 1)
                    if kind == "gate" and c:
                        hidden_turn(i, c - 1)
                    if kind == "up" and c == 1:
                        pe.wait_ge(pick_set, 4 * i + 3)
                        for tb in range(TB):
                            nc.tensor.transpose(psA[:, 1, tb * P:(tb + 1) * P], f(pick[:, tb, :]), ident[:, :])
                        for a, eq in enumerate((eqA, eqB)):
                            for tb in range(TB):
                                ins = mm(psA[:, 1, T:T + 1], eq[:, tb, :], ones[:, 0:1], start=a == 0 and tb == 0,
                                         stop=a == 1 and tb == 1)
                        ins.then_inc(pickT_mm, 1)
            for tb in range(TB):
                scatter(n, tb)


_INS = ["x", "norm_mix", "norm_ffn", "diff_w_qkv", "diff_w_o", "diff_lambda", "diff_subln", "moba_w_qkv", "moba_w_o",
        "ffn_w_gate", "ffn_w_up", "ffn_w_down", "moe_router", "moe_w_gate", "moe_w_up", "moe_w_down", "final_norm"]


def kernel(**inputs):
    import concourse.bacc as bacc
    from concourse.bass_utils import run_bass_kernel_spmd

    nc = bacc.Bacc("TRN2", target_bir_lowering=False, num_devices=1)
    arrays, args = {}, []
    for name in _INS:
        a = np.ascontiguousarray(inputs[name])
        arrays[f"in_{name}"] = a
        args.append(nc.dram_tensor(f"in_{name}", a.shape, mybir.dt.from_np(a.dtype), kind="ExternalInput").ap())
    args.append(nc.dram_tensor("out", inputs["x"].shape, F32, kind="ExternalOutput").ap())
    trunk(nc, *args)
    return run_bass_kernel_spmd(nc, [arrays], core_ids=[0]).results[0]["out"]
```

```python
import math
from contextlib import ExitStack

import numpy as np
import concourse.bass as bass
from concourse import mybir

F32 = mybir.dt.float32
F32R = mybir.dt.float32r
I32 = mybir.dt.int32
U32 = mybir.dt.uint32
ALU = mybir.AluOpType
ACT = mybir.ActivationFunctionType
AX = mybir.AxisListType

P = 128
GROUP = 512
RING = 7
HL = 6
AHEAD = 5
GS = 8
SLOT = GS * GROUP
POOL_EVERY = 4
POOL_GS = GS // POOL_EVERY
BIG = 1e30


def trunk(nc, x, norm_mix, norm_ffn, diff_w_qkv, diff_w_o, diff_lambda, diff_subln, moba_w_qkv, moba_w_o,
          ffn_w_gate, ffn_w_up, ffn_w_down, moe_router, moe_w_gate, moe_w_up, moe_w_down, final_norm, out):
    _, T, D = x.shape
    TB = T // P
    KD = D // P
    FF = ffn_w_gate.shape[2]
    E, DE = moe_w_gate.shape[1], moe_w_gate.shape[3]
    W = 512
    NF = -(-FF // W)
    NE = DE // W
    FBW = W // P
    PAIRS = D // P
    UNITS = PAIRS * TB
    EPS, SUB_EPS, SUB = 1e-6, 1e-5, 1.0 - (0.8 - 0.6 * math.exp(0.0))
    LAM_INIT = 0.8 - 0.6 * math.exp(0.0)
    SCALE = 64 ** -0.5
    assert T == 2 * P and D == 1024 and (D ** -0.5) ** 2 * D == 1.0 and DE % W == 0 and 2 * T // (P + 1) <= 3
    slopes = [[2.0 ** (-8.0 * (p + 1) / PAIRS) for p in range(PAIRS) for _ in range(2)],
              [2.0 ** (-8.0 * (h + 1) / (2 * PAIRS)) for h in range(2 * PAIRS)]]

    slots = []

    def cols(w, k, c, n):
        return w[0].rearrange("(k p) n -> p k n", p=P)[:, :, c:c + n]

    def rows(w, r, n):
        return w[0][r:r + n, :].rearrange("(g p) n -> p g n", p=P)

    first_slot = {}
    for layer, (wqkv, wo) in enumerate(((diff_w_qkv, diff_w_o), (moba_w_qkv, moba_w_o))):
        first_slot["qkv", layer] = len(slots)
        for c in (0, D, 2 * D, W, D + W, 2 * D + W):
            slots.append((cols(wqkv, KD, c, W), GS))
        first_slot["wo", layer] = len(slots)
        for r in (0, W):
            slots.append((rows(wo, r, W), GS))
        if layer == 0:
            first_slot["ffn", 0] = len(slots)
            width = [min(W, FF - c * W) for c in range(NF)]
            gate_slot, up_slot, down_slot = {}, {}, {}
            for c in range(NF + 1):
                if c < NF:
                    gate_slot[c] = len(slots)
                    slots.append((cols(ffn_w_gate, KD, c * W, width[c]), width[c] * KD // GROUP))
                    up_slot[c] = len(slots)
                    slots.append((cols(ffn_w_up, KD, c * W, width[c]), width[c] * KD // GROUP))
                if c > 0:
                    down_slot[c - 1] = len(slots)
                    slots.append((rows(ffn_w_down, (c - 1) * W, width[c - 1]), width[c - 1] // P * D // GROUP))
    NS = len(slots)
    first_group = [sum(g for _, g in slots[:s]) for s in range(NS + 1)]
    NG = first_group[NS]

    STEPS = UNITS + 2
    FILL = ([5, 3, 4, 3, 3, 3, 3, 3, 3, 2, 0, 0, 0, 1, 1, 1, 0, 0], [5, 3, 4, 3, 3, 3, 3, 3, 3, 2, 0, 0, 0, 1, 1, 1, 1, 1])
    LATE = 2
    HALF_BUILD = 12
    filled = [[first_group[first_slot["qkv", layer] + 2] + sum(FILL[layer][:t]) for t in range(STEPS + 1)]
              for layer in range(2)]
    ends = [[[s for s in range(first_slot["qkv", layer] + 2, first_slot["wo", layer])
              if filled[layer][t] < first_group[s + 1] <= filled[layer][t + 1]] for t in range(STEPS)]
            for layer in range(2)]
    assert all(filled[layer][11] == first_group[first_slot["wo", layer]] for layer in range(2))
    group_of = [(s, g) for s in range(NS) for g in range(slots[s][1])]
    by_pool = [g % POOL_EVERY == POOL_EVERY - 1 for _, g in group_of]
    pool_upto = [sum(by_pool[:n]) for n in range(NG + 1)]
    dve_upto = [n - pool_upto[n] for n in range(NG + 1)]

    item_slots = [("gate", 0), ("up", 0)]
    for c in range(1, NE):
        item_slots += [("gate", c), ("up", c), ("down", c - 1)]
    item_slots += [("down", NE - 1)]
    item_slot = {key: j for j, key in enumerate(item_slots)}
    IS = len(item_slots)
    IG = GS * IS
    LAST_TURN = GS * item_slot["down", NE - 2] + 4
    assert IS % RING == 0 and IG % HL == 0 and all(g == GS for _, g in slots[-RING:])

    with ExitStack() as ctx:
        def sb(name, shape, dt=F32, stack=ctx):
            return stack.enter_context(nc.sbuf_tensor(name, shape, dt))

        def sem(name):
            return ctx.enter_context(nc.semaphore(name))

        ring = sb("ring", [P, RING, SLOT])
        whi = sb("whi", [P, HL, GROUP], F32R)
        wlo = sb("wlo", [P, HL, GROUP], F32R)
        xhi = sb("xhi", [P, KD, T], F32R)
        xlo = sb("xlo", [P, KD, T], F32R)
        res = sb("res", [P, TB, D])
        rowbuf = sb("rowbuf", [P, TB, D])
        rt = sb("rt", [P, KD, E])
        expert_no = sb("expert_no", [P, E])
        ident = sb("ident", [P, P])
        ones = sb("ones", [P, P])
        before = sb("before", [P, P])
        slotno = sb("slotno", [P, P])
        gain_rows = sb("gain_rows", [40, P])
        gain_cols = sb("gain_cols", [P, 40])
        small = sb("small", [P, 16])
        ssq = sb("ssq", [P, 5, 2, TB])
        rstd = sb("rstd", [P, 5, TB])
        q_scale = sb("q_scale", [P, 2, PAIRS])
        halfneg = sb("halfneg", [P, 2 * PAIRS])
        score_min = sb("score_min", [P, 2, UNITS, 2])
        prob_sum = sb("prob_sum", [P, 2, UNITS, 2])
        prob_inv = sb("prob_inv", [P, 2, UNITS, 2])
        mix = sb("mix", [P, UNITS])
        head_ssq = sb("head_ssq", [P, TB, PAIRS])
        head_rstd = sb("head_rstd", [P, TB, PAIRS])

        attn = ExitStack()
        qT = sb("qT", [P, PAIRS, T], F32, attn)
        kT = sb("kT", [P, PAIRS, T], F32, attn)
        val = sb("val", [P, TB, D], F32, attn)
        probs = sb("probs", [P, 2, 2, T], F32, attn)
        lam = probs[:, 0, 0, :].rearrange("p (a d) -> p a d", a=4)
        lam_prod = probs[:, 0, 1, 0:64]
        junk = sb("junk", [P, P], F32, attn)
        probsT = sb("probsT", [P, 2, 4, P], F32, attn)
        dist = sb("dist", [P, 3 * P], F32, attn)
        attn.close()
        hidT = sb("hidT", [P, FBW, T])
        gain = hidT[:, :, :].rearrange("p b n -> p (b n)")
        hid = hidT[:, 0:2, :].rearrange("p b n -> p (b n)")
        hhi = sb("hhi", [P, FBW, T], F32R)
        hlo = sb("hlo", [P, FBW, T], F32R)
        ihi = sb("ihi", [P, KD, P], F32R)
        ilo = sb("ilo", [P, KD, P], F32R)
        yhi = sb("yhi", [P, D], F32R)
        ylo = sb("ylo", [P, D], F32R)
        pick = sb("pick", [P, TB, P], F32R)
        pickT = sb("pickT", [P, T], F32R)
        eqA = sb("eqA", [P, TB, P])
        ident_r = sb("ident_r", [P, P], F32R)
        gate_of_slot = sb("gate_of_slot", [P, 1])
        rt_hi = sb("rt_hi", [P, KD, E], F32R)
        rt_lo = sb("rt_lo", [P, KD, E], F32R)
        logit = sb("logit", [P, TB, E])
        top = sb("top", [P, TB, E])
        top_at = sb("top_at", [P, TB, E], U32)
        top_atf = sb("top_atf", [P, TB, E])
        logitT = sb("logitT", [E, T])
        count = hlo[:, 0, :].rearrange("p (a t) -> p a t", a=2)
        chosen = sb("chosen", [P, 2, TB, E])
        member = sb("member", [P, TB, E], F32R)
        pos = sb("pos", [P, 3, E])
        over = sb("over", [P, 5 + E])
        over2 = sb("over2", [P, 2 + E])
        over4 = sb("over4", [P, 4 + E])
        over_before = sb("over_before", [P, E])
        far = sb("far", [P, TB, E])
        jump = sb("jump", [P, E])
        key_jump = sb("key_jump", [P, 2, TB])
        jump_base = sb("jump_base", [P, E])
        first_place = sb("first_place", [P, E])
        place = sb("place", [P, TB, E])
        taken = sb("taken", [P, 2, TB, E])
        hit = sb("hit", [P, 3, E])
        key = sb("key", [P, 2, TB])
        wgt = sb("wgt", [P, 2, TB])
        first_wgt = sb("first_wgt", [P, TB])
        wtmp = sb("wtmp", [P, 2, TB])
        extra_f = sb("extra_f", [P, 4])
        extra = sb("extra", [P, 4], I32)

        psA = ctx.enter_context(nc.psum_tensor("psA", [P, 2, W], F32))
        psB = ctx.enter_context(nc.psum_tensor("psB", [P, 2, W], F32))
        psY = ctx.enter_context(nc.psum_tensor("psY", [P, 4, W], F32))

        x_in = [sem(f"x_in{tb}") for tb in range(TB)]
        gains_in = sem("gains_in")
        lam_in = sem("lam_in")
        gain_in = sem("gain_in")
        router_in = sem("router_in")
        first_half = sem("first_half")
        slot_full = [sem(f"slot_full{r}") for r in range(RING)]
        hi_done = sem("hi_done")
        lo_dve = sem("lo_dve")
        lo_pool = sem("lo_pool")
        group_used = sem("group_used")
        consts = sem("consts")
        gains_T = sem("gains_T")
        gains_set = sem("gains_set")
        lam_exp = sem("lam_exp")
        lam_dot = sem("lam_dot")
        ssq_done = sem("ssq_done")
        rstd_done = sem("rstd_done")
        rows_done = sem("rows_done")
        turn_done = sem("turn_done")
        xhi_done = sem("xhi_done")
        xlo_done = sem("xlo_done")
        qkv_done = sem("qkv_done")
        score_half = sem("score_half")
        score_done = sem("score_done")
        min_done = sem("min_done")
        exp_done = sem("exp_done")
        mixed = sem("mixed")
        probT_done = sem("probT_done")
        probT_out = sem("probT_out")
        pv_done = sem("pv_done")
        o_done = sem("o_done")
        o_ssq = sem("o_ssq")
        o_rstd = sem("o_rstd")
        res_done = sem("res_done")
        silu_done = sem("silu_done")
        hid_done = sem("hid_done")
        hhi_done = sem("hhi_done")
        hlo_done = sem("hlo_done")
        chain_dve = sem("chain_dve")
        chain_pool = sem("chain_pool")
        rt_split = sem("rt_split")
        logit_mm = sem("logit_mm")
        logitT_out = sem("logitT_out")
        count_set = sem("count_set")
        rowhi_done = sem("rowhi_done")
        rowlo_done = sem("rowlo_done")
        wdiff = sem("wdiff")
        wexp = sem("wexp")
        member_set = sem("member_set")
        pos_mm = sem("pos_mm")
        table_set = sem("table_set")
        wgt_set = sem("wgt_set")
        pick_set = sem("pick_set")
        gather_mm = sem("gather_mm")
        ihi_done = sem("ihi_done")
        ilo_done = sem("ilo_done")
        pickT_mm = sem("pickT_mm")
        pickT_set = sem("pickT_set")
        yhi_done = sem("yhi_done")
        ylo_done = sem("ylo_done")
        scatter_mm = sem("scatter_mm")
        add_done = sem("add_done")
        m_silu = sem("m_silu")
        m_hid = sem("m_hid")
        m_hidT = sem("m_hidT")
        m_hhi = sem("m_hhi")
        m_hlo = sem("m_hlo")
        out_rows = sem("out_rows")
        stored = sem("stored")

        block = ctx.enter_context(nc.Block())

        def repeat(ap, dim, n):
            layout = [list(d) for d in ap.ap]
            return bass.AP(ap.tensor, ap.offset, layout[:dim] + [[0, n]] + layout[dim:])

        def row_part(t, tb, half):
            return t[:, :, :].rearrange("p k t -> p (k t)")[:, tb * D + half * W:tb * D + (half + 1) * W]

        def place_of(c):
            return slice(c % 2 * P, c % 2 * P + P)

        def flat(t, w):
            return t[:, :, :].rearrange("p b n -> p (b n)")[:, 0:w * TB]

        def hid_parts(c):
            if c % 2 == 0:
                return hhi, hlo
            return [t[:, :, :].rearrange("p (b a) n -> p b (a n)", a=2) for t in (ihi, ilo)]

        def f(ap):
            return ap.bitcast(F32)

        def ring_group(s, g):
            return ring[:, s % RING, g * GROUP:(g + 1) * GROUP]

        def wait_group(eng, n):
            if by_pool[n]:
                eng.wait_ge(lo_pool, pool_upto[n + 1])
            else:
                eng.wait_ge(lo_dve, dve_upto[n + 1])

        def n_items(eng):
            eng.wait_ge(table_set, 1)
            return eng.value_load(extra[0:1, 0:1], min_val=0, max_val=3) + E

        def slot_landed(i, j):
            r = (NS + j) % RING
            dense = sum(1 for s in range(NS) if s % RING == r)
            return i * (16 * IS // RING) + 16 * (dense + j // RING + 1)

        def used_at(i, m):
            return i * IG + (NG + m)

        def wait_item_group(eng, i, m):
            pool_m, rest = divmod(m, POOL_EVERY)
            if rest == POOL_EVERY - 1:
                eng.wait_ge(lo_pool, i * (IG // POOL_EVERY) + (pool_upto[NG] + pool_m + 1))
            else:
                eng.wait_ge(lo_dve, i * (IG - IG // POOL_EVERY) + (dve_upto[NG] + m - pool_m + 1))

        BUILDS = [("norm", 0), ("attn", 0), ("norm", 1), ("norm", 2), ("attn", 1), ("norm", 3)]
        ROWS_BEFORE = [0, 2, 4, 6, None, 8]
        GAIN_ROW = (0, 2 * KD, KD, 3 * KD)
        PARTS = [(half, tb) for half in range(2) for tb in range(TB)]
        ROWS_GAINED = 11

        def turned(b, q):
            if BUILDS[b][0] == "norm":
                return psY[:, q, :]
            return psA[:, q, :] if q < 2 else psY[:, q - 2, :]

        @block.sync
        def _(sp):
            for tb in range(TB):
                sp.dma_start(res[:, tb, :], x[0, tb * P:(tb + 1) * P, :]).then_inc(x_in[tb], 16)
            sp.dma_start(gain_rows[0:2 * KD, :], norm_mix.rearrange("l (k p) -> (l k) p", p=P)).then_inc(gains_in, 16)
            sp.dma_start(gain_rows[2 * KD:4 * KD, :], norm_ffn.rearrange("l (k p) -> (l k) p", p=P)).then_inc(gains_in, 16)
            sp.dma_start(gain_rows[4 * KD:4 * KD + 1, :], diff_subln[:, :]).then_inc(gains_in, 16)

            for s, (src, groups) in enumerate(slots):
                if s == 2:
                    sp.dma_start(lam, diff_lambda[0].partition_broadcast(P)).then_inc(lam_in, 16)
                    sp.dma_start(rt[:, :, :], moe_router[0].rearrange("(k p) e -> p k e", p=P)).then_inc(router_in, 16)
                if s >= RING:
                    n = first_group[s - RING + 1]
                    sp.wait_ge(lo_dve, dve_upto[n])
                    sp.wait_ge(lo_pool, pool_upto[n])
                dst = ring[:, s % RING, 0:groups * GROUP].rearrange("p (k n) -> p k n", n=src.shape[2])
                if s == 0:
                    sp.dma_start(dst[:, 0:KD // 2, :], src[:, 0:KD // 2, :]).then_inc(first_half, 16)
                    dst, src = dst[:, KD // 2:, :], src[:, KD // 2:, :]
                sp.dma_start(dst, src).then_inc(slot_full[s % RING], 16)

            dve_past = sp.alloc_register("dve_past")
            pool_past = sp.alloc_register("pool_past")
            sp.reg_mov(dve_past, dve_upto[NG] + (GS - POOL_GS) * (1 - RING))
            sp.reg_mov(pool_past, pool_upto[NG] + POOL_GS * (1 - RING))

            def load(r, dst, src):
                sp.wait_ge(lo_dve, dve_past)
                sp.wait_ge(lo_pool, pool_past)
                sp.dma_start(dst, src).then_inc(slot_full[r], 16)
                sp.reg_add(dve_past, dve_past, GS - POOL_GS)
                sp.reg_add(pool_past, pool_past, POOL_GS)

            def item(e):
                for j, (kind, c) in enumerate(item_slots):
                    r = (NS + j) % RING
                    if kind == "down":
                        src = moe_w_down[0][e, c * W:(c + 1) * W, :].rearrange("(g p) n -> p g n", p=P)
                    else:
                        w = moe_w_gate if kind == "gate" else moe_w_up
                        src = w[0][e, :, c * W:(c + 1) * W].rearrange("(k p) n -> p k n", p=P)
                    load(r, ring[:, r, :].rearrange("p (k n) -> p k n", n=src.shape[2]), src)

            with sp.Fori(0, E) as i:
                item(i)
            n = n_items(sp)
            with sp.If(n > E):
                with sp.Fori(E, n) as i:
                    e = sp.value_load(extra[0:1, bass.ds(i - (E - 1), 1)], min_val=0, max_val=E - 1)
                    item(e)
            r = NS % RING
            load(r, ring[:, r, 0:2], moe_w_down[0][0, 0:P, 0:2])
            for tb in range(TB):
                sp.wait_ge(out_rows, tb + 1)
                sp.dma_start(out[0, tb * P:(tb + 1) * P, :], rowbuf[:, tb, :]).then_inc(stored, 16)
            sp.wait_ge(stored, 16 * TB)

        @block.scalar
        def _(act):
            split = [0]

            def split_to(n):
                for m in range(split[0], min(n, NG)):
                    s, g = group_of[m]
                    if m == 0:
                        act.wait_ge(first_half, 16)
                    elif g == (0 if s else GS // 2):
                        act.wait_ge(slot_full[s % RING], 16 * (s // RING + 1))
                    if m >= HL:
                        act.wait_ge(group_used, m - HL + 1)
                    nc.scalar.copy(whi[:, m % HL, :], ring_group(s, g)).then_inc(hi_done, 1)
                split[0] = max(split[0], min(n, NG))

            def square_sums(norm):
                for part, (half, tb) in enumerate(PARTS):
                    if norm == 0:
                        act.wait_ge(x_in[tb], 16)
                    elif norm < 4:
                        act.wait_ge(res_done, 4 * (norm - 1) + part + 1)
                    else:
                        act.wait_ge(add_done, n * TB + (part + 1))
                    cs = slice(half * W, (half + 1) * W)
                    nc.scalar.activation(rowbuf[:, tb, cs], res[:, tb, cs], ACT.Square, scale=D ** -0.5,
                                         accum_out=ssq[:, norm, half, tb:tb + 1]).then_inc(ssq_done, 1)

            def build(b, first=0, last=KD // 2):
                kind, j = BUILDS[b]
                for q in range(first, last):
                    bank = turned(b, q)
                    act.wait_ge(turn_done, 4 * b + q + 1)
                    if kind == "norm":
                        for k in range(2 * q, 2 * q + 2):
                            col = GAIN_ROW[j] + k
                            ins = nc.scalar.activation(xhi[:, k, :], bank[:, (k % 2) * T:(k % 2 + 1) * T], ACT.Copy,
                                                       scale=gain_cols[:, col:col + 1])
                    elif j == 0:
                        ins = nc.scalar.activation(xhi[:, 2 * q:2 * q + 2, :], bank, ACT.Copy,
                                                   scale=gain_cols[:, 4 * KD:4 * KD + 1])
                    else:
                        ins = nc.scalar.copy(xhi[:, 2 * q:2 * q + 2, :], bank)
                    ins.then_inc(xhi_done, 1)

            def exps(layer, u):
                n = UNITS * layer + u
                keys = (u % TB + 1) * P
                if u >= 2:
                    act.wait_ge(probT_done, n - 1)
                act.wait_ge(min_done, n + 1)
                for i in range(2):
                    ins = nc.scalar.activation(probs[:, u % 2, i, 0:keys], psY[:, u % 2, i * T:i * T + keys], ACT.Exp,
                                               scale=-1.0, bias=score_min[:, layer, u, i:i + 1],
                                               accum_out=prob_sum[:, layer, u, i:i + 1])
                ins.then_inc(exp_done, 1)

            def copy_probT(layer, u):
                n = UNITS * layer + u
                blocks = (u % TB + 1) * (1 if layer == 0 else 2)
                act.wait_ge(probT_done, n + 1)
                if u >= 2:
                    act.wait_ge(pv_done, n - 1)
                nc.scalar.copy(probsT[:, u % 2, 0:blocks, :], psY[:, 2, 0:blocks * P]).then_inc(probT_out, 1)

            def head_square(u):
                pair, tb = u // TB, u % TB
                at = tb * (PAIRS // 2) + pair % (PAIRS // 2)
                act.wait_ge(o_done, u + 1)
                if u >= 1:
                    act.wait_ge(o_ssq, u)
                nc.scalar.activation(junk[:, :], rowbuf[:, tb, pair * P:(pair + 1) * P], ACT.Square,
                                     accum_out=head_ssq[:, pair // (PAIRS // 2), at:at + 1]).then_inc(o_ssq, 1)

            def copy_out(layer, j):
                half, kind = divmod(j, 3)
                act.wait_ge(group_used, first_group[first_slot["qkv", layer] + j + 1])
                ps = psA if j % 2 == 0 else psB
                if kind == 0:
                    for b in range(4):
                        pair = 4 * half + b
                        ins = nc.scalar.activation(qT[:, pair, :], ps[:, b // 2, (b % 2) * T:(b % 2 + 1) * T],
                                                   ACT.Copy, scale=q_scale[:, layer, pair:pair + 1])
                elif kind == 1:
                    ins = nc.scalar.copy(kT[:, 4 * half:4 * half + 4, :], ps[:, :, :])
                else:
                    ins = nc.scalar.copy(val[:, :, half * W:(half + 1) * W], ps[:, :, :])
                ins.then_inc(qkv_done, 1)

            square_sums(0)
            act.wait_ge(gains_set, 1)
            for layer in range(2):
                if layer == 1:
                    square_sums(2)
                for q in range(KD // 2):
                    build(3 * layer, q, q + 1)
                    split_to(first_group[first_slot["qkv", layer]] + q + 1)
                s0 = first_slot["qkv", layer]
                for j in range(2):
                    split_to(first_group[s0 + j + 1] + AHEAD)
                    copy_out(layer, j)
                if layer == 0:
                    act.wait_ge(lam_dot, 1)
                    nc.scalar.activation(small[:, 2:4], small[:, 0:2], ACT.Exp).then_inc(lam_exp, 1)
                for t in range(STEPS):
                    if layer == 0 and t >= 3:
                        head_square(t - 3)
                    if t < UNITS:
                        exps(layer, t)
                    if t == HALF_BUILD:
                        build(3 * layer + 1, 0, 2)
                    split_to(filled[layer][t] + AHEAD + FILL[layer][t] // 2)
                    if 1 <= t <= UNITS:
                        copy_probT(layer, t - 1)
                    split_to(filled[layer][t + 1] + AHEAD)
                    for s in ends[layer][t]:
                        copy_out(layer, s - s0)
                if layer == 0:
                    head_square(UNITS - 1)
                split_to(first_group[first_slot["wo", layer] + 1] - LATE + AHEAD)
                build(3 * layer + 1, 2, 4)
                if layer == 1:
                    act.dma_start(gain, norm_ffn[1].partition_broadcast(P)).then_inc(gain_in, 16)
                split_to(first_group[first_slot["wo", layer] + 2] + AHEAD)
                square_sums(2 * layer + 1)
                if layer == 0:
                    build(2)
                    for c in range(NF):
                        w = width[c]
                        split_to(first_group[gate_slot[c] + 1] + AHEAD)
                        act.wait_ge(group_used, first_group[gate_slot[c] + 1])
                        if c:
                            act.wait_ge(hlo_done, c)
                        nc.scalar.activation(flat(hidT, w), psA.rearrange("p b n -> p (b n)")[:, 0:w * TB],
                                             ACT.Silu).then_inc(silu_done, 1)
                        last = down_slot[c - 1] if 0 < c < NF - 1 else up_slot[c]
                        split_to(first_group[last + 1] + AHEAD)
                        act.wait_ge(hid_done, c + 1)
                        if c >= 2:
                            act.wait_ge(group_used, first_group[down_slot[c - 2] + 1])
                        nc.scalar.copy(flat(hid_parts(c)[0], w), flat(hidT, w)).then_inc(hhi_done, 1)
                    split_to(first_group[first_slot["qkv", 1]] + AHEAD)

            act.wait_ge(router_in, 16)
            nc.scalar.copy(rt_hi[:, :, :], rt[:, :, :]).then_inc(rt_split, 1)
            nc.scalar.copy(ident_r[:, :], ident[:, :])
            nc.scalar.copy(count[:, 0, :], ones[:, :])
            nc.scalar.copy(count[:, 1, :], before[:, :]).then_inc(count_set, 1)
            build(5)
            for half in range(2):
                act.wait_ge(rows_done, ROWS_GAINED + half)
                act.wait_ge(logit_mm, 1)
                if half == 1:
                    act.wait_ge(wdiff, 1)
                    nc.scalar.activation(wtmp[:, 0, :], wtmp[:, 1, :], ACT.Exp).then_inc(wexp, 1)
                for tb in range(TB):
                    nc.scalar.copy(row_part(xhi, tb, half), rowbuf[:, tb, half * W:(half + 1) * W]).then_inc(rowhi_done, 1)

            def item_split(i, first, last):
                for m in range(first, last):
                    j, g = m // GS, m % GS
                    r = (NS + j) % RING
                    if g == 0:
                        act.wait_ge(slot_full[r], slot_landed(i, j))
                    act.wait_ge(group_used, used_at(i, m - HL + 1))
                    nc.scalar.copy(whi[:, (NG + m) % HL, :], ring[:, r, g * GROUP:(g + 1) * GROUP]).then_inc(hi_done, 1)

            def gather_hi(i, q):
                act.wait_ge(gather_mm, 2 * i + (q + 1))
                nc.scalar.copy(ihi[:, 4 * q:4 * q + 4, :], psY[:, 2 + q, :]).then_inc(ihi_done, 1)

            def hidden_hi(i, c):
                act.wait_ge(m_hidT, i * NE + (c + 1))
                nc.scalar.copy(hhi[:, :, place_of(c)], psB[:, 1, :].rearrange("p (b t) -> p b t", t=P)).then_inc(m_hhi, 1)

            nc.scalar.activation(small[:, 8:9], ones[:, 0:1], ACT.Silu)
            item_split(0, 0, AHEAD)
            gather_hi(0, 0)
            n = n_items(act)
            with act.Fori(0, n) as i:
                done = AHEAD
                for c in range(NE):
                    stop = GS * (item_slot["gate", c] + 1) + AHEAD
                    if c == 0:
                        item_split(i, done, GS)
                        gather_hi(i, 1)
                        done = GS
                    item_split(i, done, stop)
                    done = stop
                    if c:
                        hidden_hi(i, c - 1)
                    act.wait_ge(group_used, used_at(i, stop - AHEAD))
                    nc.scalar.activation(hid, psA[:, 0, :], ACT.Silu).then_inc(m_silu, 1)
                stop = LAST_TURN + AHEAD
                item_split(i, done, stop)
                hidden_hi(i, NE - 1)
                gather_hi(i + 1, 0)
                item_split(i, stop, IG)
                item_split(i + 1, 0, AHEAD)
                act.wait_ge(pickT_set, 2 * i + 2)
                for half in range(2):
                    act.wait_ge(group_used, used_at(i, IG - 1 + half))
                    nc.scalar.activation(yhi[:, half * W:(half + 1) * W], psY[:, half, :], ACT.Copy,
                                         scale=gate_of_slot[:, 0:1]).then_inc(yhi_done, 1)
            act.dma_start(gain, final_norm.partition_broadcast(P)).then_inc(gain_in, 16)
            square_sums(4)

        @block.gpsimd
        def _(pool):
            links = [0]

            def link(ins):
                links[0] += 1
                ins.then_inc(chain_pool, 1)
                pool.wait_ge(chain_pool, links[0])

            def select(ap, fill, op, base, pattern, per_row):
                return nc.gpsimd.affine_select(out=ap, in_=ap, compare_op=op, fill=fill, base=base,
                                               pattern=pattern, channel_multiplier=per_row)

            nc.gpsimd.memset(halfneg[:, :], -0.5)
            link(nc.gpsimd.memset(ident[:, :], 0.0))
            link(select(ident[:, :], 1.0, ALU.not_equal, 0, [[-1, P]], 1))
            nc.gpsimd.memset(ones[:, :], 1.0)
            link(nc.gpsimd.memset(before[:, :], 1.0))
            link(select(before[:, :], 0.0, ALU.is_gt, 0, [[1, P]], -1))
            nc.gpsimd.iota(slotno[:, :], pattern=[[1, P]], base=0, channel_multiplier=0,
                           allow_small_or_imprecise_dtypes=True)
            nc.gpsimd.iota(expert_no[:, :], pattern=[[1, E]], base=0, channel_multiplier=0,
                           allow_small_or_imprecise_dtypes=True)
            nc.gpsimd.iota(dist[:, 0:P], pattern=[[-1, P]], base=0, channel_multiplier=1,
                           allow_small_or_imprecise_dtypes=True)
            link(nc.gpsimd.iota(dist[:, P:3 * P], pattern=[[-1, T]], base=P, channel_multiplier=1,
                                allow_small_or_imprecise_dtypes=True))
            link(select(dist[:, 0:P], BIG, ALU.is_ge, 0, [[-1, P]], 1))
            select(dist[:, P:3 * P], BIG, ALU.is_ge, P, [[-1, T]], 1).then_inc(consts, 1)

            halved = [0]

            def halve_to(n):
                for m in range(halved[0], min(n, NG)):
                    if by_pool[m]:
                        s, g = group_of[m]
                        pool.wait_ge(hi_done, m + 1)
                        nc.gpsimd.tensor_tensor(wlo[:, m % HL, :], ring_group(s, g), f(whi[:, m % HL, :]),
                                                ALU.subtract).then_inc(lo_pool, 1)
                halved[0] = max(halved[0], min(n, NG))

            def root(norm):
                for tb in range(TB):
                    at = rstd[:, norm, tb:tb + 1]
                    pool.wait_ge(ssq_done, 4 * norm + PARTS.index((0, tb)) + 1)
                    link(nc.gpsimd.tensor_scalar(at, ssq[:, norm, 0, tb:tb + 1], EPS, None, ALU.add))
                    pool.wait_ge(ssq_done, 4 * norm + PARTS.index((1, tb)) + 1)
                    link(nc.gpsimd.tensor_tensor(at, at, ssq[:, norm, 1, tb:tb + 1], ALU.add))
                    nc.gpsimd.tensor_tensor(at, at, halfneg[:, 0:1], ALU.pow).then_inc(rstd_done, 1)

            root(0)
            for half in range(2):
                if half == 0:
                    halve_to(filled[0][UNITS // 2 + 2] + AHEAD)
                else:
                    halve_to(first_group[first_slot["wo", 0] + 1])
                pool.wait_ge(o_ssq, (half + 1) * UNITS // 2)
                at = head_rstd[:, half, :]
                link(nc.gpsimd.tensor_scalar(at, head_ssq[:, half, :], 1.0 / P, SUB_EPS, ALU.mult, ALU.add))
                nc.gpsimd.tensor_tensor(at, at, halfneg[:, 0:PAIRS], ALU.pow).then_inc(o_rstd, 1)
            halve_to(first_group[first_slot["ffn", 0]] + HL)
            root(1)
            halve_to(first_group[first_slot["qkv", 1]] + HL)
            root(2)
            halve_to(NG)
            root(3)
            nc.gpsimd.memset(f(pickT[:, :]), 0.0)
            nc.gpsimd.memset(f(yhi[:, :]), 0.0)
            nc.gpsimd.memset(f(ylo[:, :]), 0.0).then_inc(ylo_done, 2)
            for part, (half, tb) in enumerate(PARTS):
                pool.wait_ge(rowhi_done, part + 1)
                nc.gpsimd.tensor_tensor(row_part(xlo, tb, half), rowbuf[:, tb, half * W:(half + 1) * W],
                                        f(row_part(xhi, tb, half)), ALU.subtract).then_inc(rowlo_done, 1)
            n = n_items(pool)
            with pool.Fori(0, n) as i:
                for m in range(POOL_EVERY - 1, IG, POOL_EVERY):
                    j, g = m // GS, m % GS
                    pool.wait_ge(hi_done, used_at(i, m + 1))
                    nc.gpsimd.tensor_tensor(wlo[:, (NG + m) % HL, :], ring[:, (NS + j) % RING, g * GROUP:(g + 1) * GROUP],
                                            f(whi[:, (NG + m) % HL, :]), ALU.subtract).then_inc(lo_pool, 1)
            root(4)

        @block.vector
        def _(dve):
            links = [0]

            def link(ins):
                links[0] += 1
                ins.then_inc(chain_dve, 1)
                dve.wait_ge(chain_dve, links[0])

            halved = [0]

            def halve_to(n):
                for m in range(halved[0], min(n, NG)):
                    if not by_pool[m]:
                        s, g = group_of[m]
                        dve.wait_ge(hi_done, m + 1)
                        nc.vector.tensor_tensor(wlo[:, m % HL, :], ring_group(s, g), f(whi[:, m % HL, :]),
                                                ALU.subtract).then_inc(lo_dve, 1)
                halved[0] = max(halved[0], min(n, NG))

            def norm_diag(norm):
                for tb in range(TB):
                    dve.wait_ge(rstd_done, TB * norm + tb + 1)
                    nc.vector.tensor_scalar(rowbuf[:, tb, 0:P], ident[:, :], rstd[:, norm, tb:tb + 1], None,
                                            ALU.mult).then_inc(rows_done, 1)

            def build(b, first=0, last=KD // 2):
                kind, j = BUILDS[b]
                for q in range(first, last):
                    bank = turned(b, q)
                    dve.wait_ge(xhi_done, 4 * b + q + 1)
                    if kind == "norm":
                        for k in range(2 * q, 2 * q + 2):
                            col = GAIN_ROW[j] + k
                            ins = nc.vector.scalar_tensor_tensor(
                                out=xlo[:, k, :], in0=bank[:, (k % 2) * T:(k % 2 + 1) * T],
                                scalar=gain_cols[:, col:col + 1], in1=f(xhi[:, k, :]), op0=ALU.mult, op1=ALU.subtract)
                    else:
                        hi = f(xhi[:, 2 * q:2 * q + 2, :]).rearrange("p k t -> p (k t)")
                        lo = xlo[:, 2 * q:2 * q + 2, :].rearrange("p k t -> p (k t)")
                        if j == 0:
                            ins = nc.vector.scalar_tensor_tensor(
                                out=lo, in0=bank, scalar=gain_cols[:, 4 * KD:4 * KD + 1], in1=hi,
                                op0=ALU.mult, op1=ALU.subtract)
                        else:
                            ins = nc.vector.tensor_tensor(lo, bank, hi, ALU.subtract)
                    ins.then_inc(xlo_done, 1)

            def minima(layer, u):
                n = UNITS * layer + u
                keys = (u % TB + 1) * P
                d = dist[:, 0:P] if u % TB == 0 else dist[:, P:3 * P]
                dve.wait_ge(score_done, n + 1)
                for i in range(2):
                    s = psY[:, u % 2, i * T:i * T + keys]
                    ins = nc.vector.tensor_tensor_reduce(
                        out=s, in0=s, in1=d, scale=slopes[layer][2 * (u // TB) + i], scalar=3e38, op0=ALU.add,
                        op1=ALU.min, accum_out=score_min[:, layer, u, i:i + 1])
                ins.then_inc(min_done, 1)

            def combine(u):
                keys = (u % TB + 1) * P
                dve.wait_ge(exp_done, u + 1)
                link(nc.vector.reciprocal(prob_inv[:, 0, u, :], prob_sum[:, 0, u, :]))
                link(nc.vector.tensor_scalar(mix[:, u:u + 1], prob_sum[:, 0, u, 0:1], prob_inv[:, 0, u, 1:2],
                                             small[:, 4:5], ALU.mult, ALU.mult))
                nc.vector.scalar_tensor_tensor(
                    out=probs[:, u % 2, 0, 0:keys], in0=probs[:, u % 2, 1, 0:keys], scalar=mix[:, u:u + 1],
                    in1=probs[:, u % 2, 0, 0:keys], op0=ALU.mult, op1=ALU.add).then_inc(mixed, 1)

            def invert(u):
                dve.wait_ge(exp_done, UNITS + u + 1)
                nc.vector.reciprocal(prob_inv[:, 1, u, :], prob_sum[:, 1, u, :]).then_inc(mixed, 1)

            def output_rows(layer, u):
                pair, tb = u // TB, u % TB
                dve.wait_ge(pv_done, UNITS * layer + u + 1)
                rows_ = rowbuf[:, tb, pair * P:(pair + 1) * P]
                if layer == 0:
                    nc.vector.tensor_scalar(rows_, psY[:, 3, 0:P], prob_inv[:, 0, u, 0:1], None,
                                            ALU.mult).then_inc(o_done, 1)
                else:
                    dve.wait_ge(mixed, UNITS + u + 1)
                    nc.vector.tensor_tensor(rows_.rearrange("p (i d) -> p i d", i=2),
                                            psY[:, 3, 0:P].rearrange("p (i d) -> p i d", i=2),
                                            repeat(prob_inv[:, 1, u, :], 2, 64), ALU.mult).then_inc(o_done, 1)

            def norm_heads(half):
                dve.wait_ge(o_rstd, half + 1)
                for tb in range(TB):
                    rows_ = rowbuf[:, tb, half * W:(half + 1) * W].rearrange("p (h d) -> p h d", d=P)
                    factor = head_rstd[:, half, tb * (PAIRS // 2):(tb + 1) * (PAIRS // 2)]
                    ins = nc.vector.tensor_tensor(rows_, rows_, repeat(factor, 2, P), ALU.mult)
                ins.then_inc(rows_done, 1)

            def update_residual(end, bank):
                halve_to(end + AHEAD - 1)
                for half in range(2):
                    dve.wait_ge(group_used, end - 1 + half)
                    for tb in range(TB):
                        r = res[:, tb, half * W:(half + 1) * W]
                        nc.vector.tensor_tensor(r, bank(tb, half), r, ALU.add).then_inc(res_done, 1)

            for layer in range(2):
                for pair in range(PAIRS):
                    for i in range(2):
                        nc.vector.memset(q_scale[64 * i:64 * i + 64, layer, pair:pair + 1],
                                         -SCALE / slopes[layer][2 * pair + i])
            dve.wait_ge(consts, 1)
            norm_diag(0)
            dve.wait_ge(gains_T, 1)
            nc.vector.tensor_copy(gain_cols[:, 0:4 * KD], psA[:, 0, 0:4 * KD])
            nc.vector.tensor_scalar(gain_cols[:, 4 * KD:4 * KD + 1], psA[:, 0, 4 * KD:4 * KD + 1], SUB, None,
                                    ALU.mult).then_inc(gains_set, 1)
            for layer in range(2):
                for q in range(KD // 2):
                    build(3 * layer, q, q + 1)
                    halve_to(first_group[first_slot["qkv", layer]] + q + 1)
                halve_to(filled[layer][0] + AHEAD)
                if layer == 0:
                    dve.wait_ge(lam_in, 16)
                    for i in range(2):
                        ins = nc.vector.tensor_tensor_reduce(
                            out=lam_prod, in0=lam[:, 2 * i, :], in1=lam[:, 2 * i + 1, :], scale=1.0, scalar=0.0,
                            op0=ALU.mult, op1=ALU.add, accum_out=small[:, i:i + 1])
                        if i == 0:
                            link(ins)
                    ins.then_inc(lam_dot, 1)
                    dve.wait_ge(lam_exp, 1)
                    link(nc.vector.tensor_tensor(small[:, 5:6], small[:, 3:4], small[:, 2:3], ALU.subtract))
                    link(nc.vector.tensor_scalar(small[:, 4:5], small[:, 5:6], -LAM_INIT, None, ALU.add))
                for t in range(STEPS):
                    if t < UNITS:
                        minima(layer, t)
                    if 1 <= t <= UNITS:
                        if layer == 0:
                            combine(t - 1)
                        else:
                            invert(t - 1)
                    if layer == 0 and t == HALF_BUILD - 1:
                        norm_heads(0)
                    if t == HALF_BUILD:
                        build(3 * layer + 1, 0, 2)
                    halve_to(filled[layer][t] + AHEAD + FILL[layer][t] // 2)
                    if t >= 2:
                        output_rows(layer, t - 2)
                    halve_to(filled[layer][t + 1] + AHEAD)
                if layer == 0:
                    norm_heads(1)
                halve_to(first_group[first_slot["wo", layer] + 1] - LATE + AHEAD)
                build(3 * layer + 1, 2, 4)
                end = first_group[first_slot["wo", layer] + 2]
                update_residual(end, lambda tb, half: (psA, psB)[tb][:, half, :])
                if layer == 1:
                    break
                norm_diag(1)
                build(2)
                for c in range(NF):
                    w = width[c]
                    halve_to(first_group[up_slot[c] + 1] + AHEAD)
                    dve.wait_ge(silu_done, c + 1)
                    dve.wait_ge(group_used, first_group[up_slot[c] + 1])
                    nc.vector.tensor_tensor(flat(hidT, w), psB.rearrange("p b n -> p (b n)")[:, 0:w * TB], flat(hidT, w),
                                            ALU.mult).then_inc(hid_done, 1)
                    last = down_slot[c - 1] if 0 < c < NF - 1 else up_slot[c]
                    halve_to(first_group[last + 1] + AHEAD)
                    dve.wait_ge(hhi_done, c + 1)
                    hi, lo = hid_parts(c)
                    nc.vector.tensor_tensor(flat(lo, w), flat(hidT, w), f(flat(hi, w)), ALU.subtract).then_inc(hlo_done, 1)
                end = first_group[first_slot["qkv", 1]]
                update_residual(end, lambda tb, half: psY[:, 2 * tb + half, :])
                norm_diag(2)

            dve.wait_ge(rt_split, 1)
            nc.vector.tensor_tensor(rt_lo[:, :, :], rt[:, :, :], f(rt_hi[:, :, :]), ALU.subtract).then_inc(rt_split, 1)
            norm_diag(3)
            build(5)
            nc.vector.tensor_scalar(first_place[:, :], expert_no[:, :], float(P), None, ALU.mult)
            nc.vector.tensor_scalar(jump_base[:, :], expert_no[:, :], -float(P), float(P * (E - 1)), ALU.mult, ALU.add)
            nc.vector.memset(over[:, 0:5], 0.0)
            nc.vector.memset(over2[:, 0:2], 0.0)
            link(nc.vector.memset(over4[:, 0:4], 0.0))

            def expert_rows(half):
                ws = slice(half * W, (half + 1) * W)
                for tb in range(TB):
                    ins = nc.vector.scalar_tensor_tensor(
                        out=rowbuf[:, tb, ws], in0=res[:, tb, ws], scalar=rstd[:, 3, tb:tb + 1], in1=gain[:, ws],
                        op0=ALU.mult, op1=ALU.mult)
                ins.then_inc(rows_done, 1)

            dve.wait_ge(gain_in, 16)
            dve.wait_ge(turn_done, 4 * 6)
            expert_rows(0)
            dve.wait_ge(logit_mm, 1)
            nc.vector.tensor_copy(logitT[:, :], psA[0:E, 0, 0:T]).then_inc(logitT_out, 1)
            dve.wait_ge(logit_mm, 2)
            link(nc.vector.tensor_copy(logit[:, :, :], psA[:, 1, 0:TB * E].rearrange("p (b e) -> p b e", e=E)))
            for tb in range(TB):
                ins = nc.vector.max(top[:, tb, :], logit[:, tb, :])
            link(ins)
            for tb in range(TB):
                ins = nc.vector.max_index(top_at[:, tb, :], top[:, tb, :], logit[:, tb, :])
            link(ins)
            nc.vector.tensor_tensor(wtmp[:, 1, :], top[:, :, 1], top[:, :, 0], ALU.subtract).then_inc(wdiff, 1)
            link(nc.vector.tensor_copy(top_atf[:, :, :], top_at[:, :, :]))
            link(nc.vector.tensor_tensor(chosen[:, :, :, :], repeat(repeat(expert_no[:, :], 1, TB), 1, 2),
                                         repeat(top_atf[:, :, 0:2].rearrange("p b a -> p a b"), 3, E), ALU.is_equal))
            nc.vector.tensor_tensor(member[:, :, :], chosen[:, 0, :, :], chosen[:, 1, :, :], ALU.add).then_inc(member_set, 1)
            expert_rows(1)
            dve.wait_ge(pos_mm, 1)
            link(nc.vector.tensor_copy(pos[:, :, :], psA[:, 0, 0:3 * E].rearrange("p (b e) -> p b e", e=E)))
            link(nc.vector.tensor_tensor(place[:, :, :], pos[:, 0:TB, :], repeat(first_place[:, :], 1, TB), ALU.add))
            link(nc.vector.tensor_tensor(taken[:, :, :, :], chosen[:, :, :, :], repeat(place[:, :, :], 1, 2), ALU.mult))
            link(nc.vector.tensor_reduce(out=key[:, :, :], in_=taken[:, :, :, :], axis=AX.X, op=ALU.add))

            def first_one_hots(i):
                for tb in range(TB):
                    ins = nc.vector.tensor_scalar(eqA[:, tb, :], slotno[:, :], key[:, 0, tb:tb + 1], None, ALU.is_equal)
                ins.then_inc(pick_set, 1)

            def one_hots(i):
                dve.wait_ge(pick_set, 3 * i + 1)
                for tb in range(TB):
                    ins = nc.vector.scalar_tensor_tensor(
                        out=pick[:, tb, :], in0=slotno[:, :], scalar=key[:, 1, tb:tb + 1], in1=eqA[:, tb, :],
                        op0=ALU.is_equal, op1=ALU.add)
                ins.then_inc(pick_set, 1)
                dve.wait_ge(pick_set, 3 * i + 2)
                nc.vector.tensor_scalar(key[:, :, :], key[:, :, :], -float(P), None, ALU.add).then_inc(pick_set, 1)
                dve.wait_ge(pick_set, 3 * i + 3)

            def item_halve(i, first, last):
                for m in range(first, last):
                    if m % POOL_EVERY != POOL_EVERY - 1:
                        dve.wait_ge(hi_done, used_at(i, m + 1))
                        g = m % GS
                        nc.vector.tensor_tensor(
                            wlo[:, (NG + m) % HL, :], ring[:, (NS + m // GS) % RING, g * GROUP:(g + 1) * GROUP],
                            f(whi[:, (NG + m) % HL, :]), ALU.subtract).then_inc(lo_dve, 1)

            def gather_lo(i, q):
                dve.wait_ge(ihi_done, 2 * i + (q + 1))
                nc.vector.tensor_tensor(
                    ilo[:, 4 * q:4 * q + 4, :].rearrange("p k t -> p (k t)"), psY[:, 2 + q, :],
                    f(ihi[:, 4 * q:4 * q + 4, :]).rearrange("p k t -> p (k t)"), ALU.subtract).then_inc(ilo_done, 1)

            def hidden_lo(i, c):
                dve.wait_ge(m_hhi, i * NE + (c + 1))
                nc.vector.tensor_tensor(hlo[:, :, place_of(c)], psB[:, 1, :].rearrange("p (b t) -> p b t", t=P),
                                        f(hhi[:, :, place_of(c)]), ALU.subtract).then_inc(m_hlo, 1)

            def add_scattered(i, tb):
                dve.wait_ge(scatter_mm, TB * i + (tb + 1))
                r = res[:, tb, :]
                nc.vector.tensor_tensor(r, psY[:, 2:4, :].rearrange("p b n -> p (b n)"), r, ALU.add).then_inc(add_done, 1)

            first_one_hots(0)
            one_hots(0)
            link(nc.vector.tensor_scalar(over[:, 5:5 + E], pos[:, 2, :], float(P), None, ALU.is_gt))
            link(nc.vector.tensor_tensor(over2[:, 2:2 + E], over[:, 4:4 + E], over[:, 3:3 + E], ALU.add))
            link(nc.vector.tensor_tensor(over4[:, 4:4 + E], over2[:, 2:2 + E], over2[:, 0:E], ALU.add))
            link(nc.vector.tensor_tensor(over_before[:, :], over4[:, 4:4 + E], over4[:, 0:E], ALU.add))
            nc.vector.tensor_tensor(extra_f[:, 0:1], over_before[:, E - 1:E], over[:, 4 + E:5 + E], ALU.add)
            link(nc.vector.tensor_tensor(hit[:, :, :], repeat(over_before[:, :], 1, 3), repeat(slotno[:, 0:3], 2, E),
                                         ALU.is_equal))
            link(nc.vector.tensor_tensor(hit[:, :, :], hit[:, :, :], repeat(over[:, 5:5 + E], 1, 3), ALU.mult))
            link(nc.vector.tensor_tensor(hit[:, :, :], hit[:, :, :], repeat(expert_no[:, :], 1, 3), ALU.mult))
            link(nc.vector.tensor_reduce(out=extra_f[:, 1:4], in_=hit[:, :, :], axis=AX.X, op=ALU.add))
            nc.vector.tensor_copy(extra[:, :], extra_f[:, :]).then_inc(table_set, 1)
            item_halve(0, 0, AHEAD)
            gather_lo(0, 0)
            link(nc.vector.scalar_tensor_tensor(out=jump[:, :], in0=over_before[:, :], scalar=float(P),
                                                in1=jump_base[:, :], op0=ALU.mult, op1=ALU.add))
            link(nc.vector.scalar_tensor_tensor(out=far[:, :, :], in0=pos[:, 0:TB, :], scalar=float(P),
                                                in1=repeat(jump[:, :], 1, TB), op0=ALU.is_ge, op1=ALU.mult))
            link(nc.vector.tensor_tensor(taken[:, :, :, :], chosen[:, :, :, :], repeat(far[:, :, :], 1, 2), ALU.mult))
            link(nc.vector.tensor_reduce(out=key_jump[:, :, :], in_=taken[:, :, :, :], axis=AX.X, op=ALU.add))
            link(nc.vector.tensor_tensor(key[:, :, :], key[:, :, :], key_jump[:, :, :], ALU.add))
            dve.wait_ge(wexp, 1)
            link(nc.vector.tensor_scalar(wtmp[:, 1, :], wtmp[:, 0, :], 1.0, None, ALU.add))
            link(nc.vector.reciprocal(first_wgt[:, :], wtmp[:, 1, :]))
            link(nc.vector.tensor_tensor(wgt[:, 0, :], first_wgt[:, :], wtmp[:, 0, :], ALU.mult))
            nc.vector.tensor_tensor(wgt[:, 1, :], first_wgt[:, :], wgt[:, 0, :], ALU.subtract).then_inc(wgt_set, 1)
            n = n_items(dve)
            with dve.Fori(0, n) as i:
                done = AHEAD
                for c in range(NE):
                    stop = GS * (item_slot["gate", c] + 1) + AHEAD
                    if c == 0:
                        item_halve(i, done, GS)
                        gather_lo(i, 1)
                        done = GS
                    item_halve(i, done, stop)
                    if c == 0:
                        add_scattered(i, 0)
                    else:
                        hidden_lo(i, c - 1)
                    done, stop = stop, GS * (item_slot["up", c] + 1) + AHEAD
                    item_halve(i, done, stop)
                    done = stop
                    dve.wait_ge(m_silu, i * NE + (c + 1))
                    dve.wait_ge(group_used, used_at(i, stop - AHEAD))
                    nc.vector.tensor_tensor(hid, psB[:, 0, :], hid, ALU.mult).then_inc(m_hid, 1)
                    if c == 0:
                        add_scattered(i, 1)
                    if c == 2:
                        dve.wait_ge(pickT_mm, i + 1)
                        nc.vector.tensor_copy(pickT[:, :], psA[:, 1, 0:T]).then_inc(pickT_set, 1)
                        nc.vector.tensor_copy(gate_of_slot[:, :], psA[:, 1, T:T + 1]).then_inc(pickT_set, 1)
                    if c == 3:
                        first_one_hots(i + 1)
                    if c == 4:
                        one_hots(i + 1)
                stop = LAST_TURN + AHEAD
                item_halve(i, done, stop)
                hidden_lo(i, NE - 1)
                gather_lo(i + 1, 0)
                item_halve(i, stop, IG)
                item_halve(i + 1, 0, AHEAD)
                for half in range(2):
                    ws = slice(half * W, (half + 1) * W)
                    dve.wait_ge(yhi_done, 2 * i + (half + 1))
                    nc.vector.scalar_tensor_tensor(out=ylo[:, ws], in0=psY[:, half, :], scalar=gate_of_slot[:, 0:1],
                                                   in1=f(yhi[:, ws]), op0=ALU.mult, op1=ALU.subtract).then_inc(ylo_done, 1)
            for part, (half, tb) in enumerate(PARTS):
                dve.wait_ge(scatter_mm, TB * n + (part + 1))
                ps, r = psA[:, half, :] if tb else psY[:, 2 + half, :], res[:, tb, half * W:(half + 1) * W]
                nc.vector.tensor_tensor(r, ps, r, ALU.add).then_inc(add_done, 1)
            dve.wait_ge(gain_in, 32)
            for tb in range(TB):
                dve.wait_ge(rstd_done, TB * 4 + tb + 1)
                nc.vector.scalar_tensor_tensor(out=rowbuf[:, tb, :], in0=res[:, tb, :], scalar=rstd[:, 4, tb:tb + 1],
                                               in1=gain, op0=ALU.mult, op1=ALU.mult).then_inc(out_rows, 1)

        @block.tensor
        def _(pe):
            mm = nc.tensor.matmul

            def three(ps, xh, xl, wh, wl, start, stop, shared=False):
                mm(ps, xh, wh, start=start, stop=False, skip_group_check=shared)
                mm(ps, xh, wl, start=False, stop=False, skip_group_check=shared)
                return mm(ps, xl, wh, start=False, stop=stop, skip_group_check=shared)

            def build(b, first=0, last=KD // 2):
                kind, j = BUILDS[b]
                for q in range(first, last):
                    if b == 4:
                        pe.wait_ge(o_done, UNITS + (q // 2 + 1) * UNITS // 2)
                    elif kind == "attn":
                        pe.wait_ge(rows_done, ROWS_BEFORE[b] + q // 2 + 1)
                    for tb in range(TB):
                        if kind == "norm" and q == 0:
                            pe.wait_ge(rows_done, ROWS_BEFORE[b] + tb + 1)
                        for k in range(2):
                            at = turned(b, q)[:, k * T + tb * P:k * T + (tb + 1) * P]
                            chunk = slice((2 * q + k) * P, (2 * q + k + 1) * P)
                            if kind == "norm":
                                ins = mm(at, res[:, tb, chunk], rowbuf[:, tb, 0:P], start=True, stop=True)
                            else:
                                ins = nc.tensor.transpose(at, rowbuf[:, tb, chunk], ident[:, :])
                    ins.then_inc(turn_done, 1)

            def cols_group(s, g, b, ps):
                n = first_group[s] + g
                wait_group(pe, n)
                pe.wait_ge(xlo_done, 4 * b + g // 2 + 1)
                for tb in range(TB):
                    xs = slice(tb * P, (tb + 1) * P)
                    ins = three(ps[:, tb, :], xhi[:, g, xs], xlo[:, g, xs], whi[:, n % HL, :], wlo[:, n % HL, :],
                                g == 0, g == KD - 1)
                ins.then_inc(group_used, 1)

            def turned_group(s, g, b, ps, w=W):
                n, per = first_group[s] + g, GROUP // w
                wait_group(pe, n)
                for kk in range(per):
                    k = per * g + kk
                    pe.wait_ge(xlo_done, 4 * b + k // 2 + 1)
                    for fb in range(w // P):
                        ws = slice(kk * w + fb * P, kk * w + (fb + 1) * P)
                        ins = three(ps[:, fb // 2, (fb % 2) * T:(fb % 2 + 1) * T], whi[:, n % HL, ws],
                                    wlo[:, n % HL, ws], xhi[:, k, :], xlo[:, k, :],
                                    k == 0 and fb % 2 == 0, k == KD - 1, shared=True)
                ins.then_inc(group_used, 1)

            def qkv_group(layer, j, g):
                if g == 0:
                    if j >= 2:
                        pe.wait_ge(qkv_done, 6 * layer + j - 1)
                    elif layer == 0:
                        pe.wait_ge(gains_set, 1)
                (cols_group if j % 3 == 2 else turned_group)(first_slot["qkv", layer] + j, g, 3 * layer,
                                                             psA if j % 2 == 0 else psB)

            def rows_group(s, g, left, outs, first, last):
                n, (k, half) = first_group[s] + g, divmod(g, 2)
                wait_group(pe, n)
                xh, xl = left(k)
                for tb in range(TB):
                    xs = slice(tb * P, (tb + 1) * P)
                    ins = three(outs[tb][:, half, :], xh[:, xs], xl[:, xs], whi[:, n % HL, :],
                                wlo[:, n % HL, :], first and k == 0, last and g >= slots[s][1] - 2)
                ins.then_inc(group_used, 1)

            def rows_slot(s, left, outs, first, last):
                for g in range(slots[s][1]):
                    rows_group(s, g, left, outs, first, last)

            def wo_group(layer, j, g):
                def attn_left(k):
                    if j == 0 and g == 0:
                        pe.wait_ge(xlo_done, 4 * (3 * layer + 1) + 2)
                    elif j == 1:
                        pe.wait_ge(xlo_done, 4 * (3 * layer + 1) + 2 + k // 2 + 1)
                    return xhi[:, 4 * j + k, :], xlo[:, 4 * j + k, :]
                rows_group(first_slot["wo", layer] + j, g, attn_left, (psA, psB), j == 0, j == 1)

            def fill(layer, first, last):
                for n in range(first, last):
                    s, g = group_of[n]
                    if s < first_slot["wo", layer]:
                        qkv_group(layer, s - first_slot["qkv", layer], g)
                    else:
                        wo_group(layer, s - first_slot["wo", layer], g)

            def scores(layer, u):
                n, pair, tb = UNITS * layer + u, u // TB, u % TB
                keys = (tb + 1) * P
                pe.wait_ge(qkv_done, 6 * layer + (2 if pair < PAIRS // 2 else 5))
                if u >= 2:
                    pe.wait_ge(exp_done, n - 1)
                for i in range(2):
                    rows_ = slice(64 * i, 64 * i + 64)
                    ins = mm(psY[:, u % 2, i * T:i * T + keys], qT[rows_, pair, tb * P:(tb + 1) * P],
                             kT[rows_, pair, 0:keys], start=True, stop=True)
                    if i == 0:
                        ins.then_inc(score_half, 1)
                        pe.wait_ge(score_half, n + 1)
                ins.then_inc(score_done, 1)

            def turn_probs(layer, u):
                n, tb = UNITS * layer + u, u % TB
                if layer == 0:
                    pe.wait_ge(mixed, u + 1)
                else:
                    pe.wait_ge(exp_done, n + 1)
                if u >= 1:
                    pe.wait_ge(probT_out, n)
                at = 0
                for i in range(1 if layer == 0 else 2):
                    for kb in range(tb + 1):
                        ins = nc.tensor.transpose(psY[:, 2, at * P:(at + 1) * P],
                                                  probs[:, u % 2, i, kb * P:(kb + 1) * P], ident[:, :])
                        at += 1
                ins.then_inc(probT_done, 1)

            def weigh_values(layer, u):
                n, pair, tb = UNITS * layer + u, u // TB, u % TB
                pe.wait_ge(probT_out, n + 1)
                pe.wait_ge(qkv_done, 6 * layer + (3 if pair < PAIRS // 2 else 6))
                if u >= 1:
                    pe.wait_ge(o_done, n)
                heads = 1 if layer == 0 else 2
                wide = P // heads
                for i in range(heads):
                    for kb in range(tb + 1):
                        c = pair * P + i * wide
                        ins = mm(psY[:, 3, i * wide:(i + 1) * wide], probsT[:, u % 2, i * (tb + 1) + kb, :],
                                 val[:, kb, c:c + wide], start=kb == 0, stop=kb == tb)
                ins.then_inc(pv_done, 1)

            pe.wait_ge(consts, 1)
            pe.wait_ge(gains_in, 16 * 3)
            nc.tensor.transpose(psA[:, 0, 0:4 * KD + 1], gain_rows[0:4 * KD + 1, :],
                                ident[0:4 * KD + 1, 0:4 * KD + 1]).then_inc(gains_T, 1)
            for layer in range(2):
                b = 3 * layer
                build(b)
                for j in range(2):
                    for g in range(GS):
                        qkv_group(layer, j, g)
                for t in range(STEPS):
                    start, stop = filled[layer][t], filled[layer][t + 1]
                    middle = stop - FILL[layer][t] // 2
                    if t == 0:
                        fill(layer, start, start + 2)
                        start += 2
                    if t < UNITS:
                        scores(layer, t)
                    if t == HALF_BUILD:
                        build(b + 1, 0, 2)
                    if t >= 2:
                        weigh_values(layer, t - 2)
                    fill(layer, start, middle)
                    if 1 <= t <= UNITS:
                        turn_probs(layer, t - 1)
                    fill(layer, middle, stop)
                turn = first_group[first_slot["wo", layer] + 1] - LATE
                fill(layer, filled[layer][STEPS], turn)
                build(b + 1, 2, 4)
                fill(layer, turn, first_group[first_slot["wo", layer] + 2])
                if layer == 1:
                    break
                build(2)
                for c in range(NF + 1):
                    if c < NF:
                        if c:
                            pe.wait_ge(silu_done, c)
                        for g in range(slots[gate_slot[c]][1]):
                            turned_group(gate_slot[c], g, 2, psA, width[c])
                        if c:
                            pe.wait_ge(hid_done, c)
                        for g in range(slots[up_slot[c]][1]):
                            turned_group(up_slot[c], g, 2, psB, width[c])
                    if c:
                        pe.wait_ge(hlo_done, c)
                        rows_slot(down_slot[c - 1], lambda k, c=c: [part[:, k, :] for part in hid_parts(c - 1)],
                                  (psY[:, 0:2, :], psY[:, 2:4, :]), c == 1, c == NF)

            build(5)
            pe.wait_ge(rt_split, 2)
            for k in range(KD):
                pe.wait_ge(xlo_done, 4 * 5 + k // 2 + 1)
                ins = three(psA[0:E, 0, 0:T], rt_hi[:, k, :], rt_lo[:, k, :], xhi[:, k, :], xlo[:, k, :],
                            k == 0, k == KD - 1)
            ins.then_inc(logit_mm, 1)
            pe.wait_ge(logitT_out, 1)
            for tb in range(TB):
                ins = nc.tensor.transpose(psA[:, 1, tb * E:(tb + 1) * E], logitT[:, tb * P:(tb + 1) * P], ident[0:E, 0:E])
            ins.then_inc(logit_mm, 1)
            pe.wait_ge(count_set, 1)
            pe.wait_ge(member_set, 1)
            mm(psA[:, 0, 0:E], count[:, 1, :], member[:, 0, :], start=True, stop=True)
            mm(psA[:, 0, E:2 * E], count[:, 1, :], member[:, 1, :], start=True, stop=False)
            mm(psA[:, 0, E:2 * E], count[:, 0, :], member[:, 0, :], start=False, stop=True)
            mm(psA[:, 0, 2 * E:3 * E], count[:, 0, :], member[:, 0, :], start=True, stop=False)
            mm(psA[:, 0, 2 * E:3 * E], count[:, 0, :], member[:, 1, :], start=False, stop=True).then_inc(pos_mm, 1)

            rows_hi = xhi[:, :, :].rearrange("p k t -> p (k t)")
            rows_lo = xlo[:, :, :].rearrange("p k t -> p (k t)")

            def gather(i, q):
                pe.wait_ge(pick_set, 3 * i + 2)
                for k in range(4 * q, 4 * q + 4):
                    for tb in range(TB):
                        for part, rows_ in enumerate((rows_hi, rows_lo)):
                            ins = mm(psY[:, 2 + q, (k % 4) * P:(k % 4 + 1) * P],
                                     rows_[:, tb * D + k * P:tb * D + (k + 1) * P], pick[:, tb, :],
                                     start=tb == 0 and part == 0, stop=tb == TB - 1 and part == 1)
                ins.then_inc(gather_mm, 1)

            def scatter(i, tb):
                if tb == 0:
                    pe.wait_ge(ylo_done, 2 * i + 2)
                    pe.wait_ge(ilo_done, 2 * i + 2)
                else:
                    pe.wait_ge(add_done, TB * i + tb)
                for half in range(2):
                    ws = slice(half * W, (half + 1) * W)
                    mm(psY[:, 2 + half, :], pickT[:, tb * P:(tb + 1) * P], yhi[:, ws], start=True, stop=False)
                    ins = mm(psY[:, 2 + half, :], pickT[:, tb * P:(tb + 1) * P], ylo[:, ws], start=False, stop=True)
                ins.then_inc(scatter_mm, 1)

            def hidden_turn(i, c):
                pe.wait_ge(m_hid, i * NE + (c + 1))
                for fb in range(FBW):
                    ins = nc.tensor.transpose(psB[:, 1, fb * P:(fb + 1) * P], hid[:, fb * P:(fb + 1) * P], ident[:, :])
                ins.then_inc(m_hidT, 1)

            def item_slot_products(i, j):
                kind, c = item_slots[j]
                if kind == "gate" and c:
                    pe.wait_ge(m_silu, i * NE + c)
                if kind == "down":
                    pe.wait_ge(m_hlo, i * NE + (c + 1))
                for g in range(GS):
                    m = GS * j + g
                    at = (NG + m) % HL
                    wait_item_group(pe, i, m)
                    if m == LAST_TURN:
                        hidden_turn(i, NE - 1)
                        gather(i + 1, 0)
                    if j == 0 and g == 2:
                        gather(i, 1)
                    if j == 0 and g == GS // 2:
                        pe.wait_ge(ilo_done, 2 * i + 2)
                    if kind == "down":
                        k, half = divmod(g, 2)
                        ins = three(psY[:, half, :], hhi[:, k, place_of(c)], hlo[:, k, place_of(c)], whi[:, at, :], wlo[:, at, :],
                                    c == 0 and k == 0, c == NE - 1 and k == FBW - 1)
                    else:
                        ps = (psA if kind == "gate" else psB)[:, 0, :]
                        ins = three(ps, ihi[:, g, :], ilo[:, g, :], whi[:, at, :], wlo[:, at, :], g == 0, g == KD - 1)
                    ins.then_inc(group_used, 1)

            pe.wait_ge(rowlo_done, TB)
            gather(0, 0)
            pe.wait_ge(rowlo_done, 2 * TB)
            n = n_items(pe)
            with pe.Fori(0, n) as i:
                pe.wait_ge(ilo_done, 2 * i + 1)
                for j, (kind, c) in enumerate(item_slots):
                    item_slot_products(i, j)
                    if kind == "gate" and c == 0:
                        scatter(i, 0)
                    if kind == "up" and c == 0:
                        scatter(i, 1)
                    if kind == "gate" and c:
                        hidden_turn(i, c - 1)
                    if kind == "up" and c == 1:
                        pe.wait_ge(wgt_set, 1)
                        for tb in range(TB):
                            mm(psA[:, 1, tb * P:(tb + 1) * P], pick[:, tb, :], ident_r[:, :], start=True, stop=True)
                        for a, onehot in enumerate((f(pick[:, :, :]), eqA)):
                            for tb in range(TB):
                                ins = mm(psA[:, 1, T:T + 1], onehot[:, tb, :], wgt[:, a, tb:tb + 1],
                                         start=a == 0 and tb == 0, stop=a == 1 and tb == 1)
                        ins.then_inc(pickT_mm, 1)
            pe.wait_ge(ilo_done, 2 * n + 1)
            for half in range(2):
                pe.wait_ge(ylo_done, 2 * n + half + 1)
                ws = slice(half * W, (half + 1) * W)
                for tb, ps in enumerate((psY[:, 2:4, :], psA)):
                    mm(ps[:, half, :], pickT[:, tb * P:(tb + 1) * P], yhi[:, ws], start=True, stop=False)
                    mm(ps[:, half, :], pickT[:, tb * P:(tb + 1) * P], ylo[:, ws], start=False,
                       stop=True).then_inc(scatter_mm, 1)


_INS = ["x", "norm_mix", "norm_ffn", "diff_w_qkv", "diff_w_o", "diff_lambda", "diff_subln", "moba_w_qkv", "moba_w_o",
        "ffn_w_gate", "ffn_w_up", "ffn_w_down", "moe_router", "moe_w_gate", "moe_w_up", "moe_w_down", "final_norm"]


def kernel(**inputs):
    import concourse.bacc as bacc
    from concourse.bass_utils import run_bass_kernel_spmd

    nc = bacc.Bacc("TRN2", target_bir_lowering=False, num_devices=1)
    arrays, args = {}, []
    for name in _INS:
        a = np.ascontiguousarray(inputs[name])
        arrays[f"in_{name}"] = a
        args.append(nc.dram_tensor(f"in_{name}", a.shape, mybir.dt.from_np(a.dtype), kind="ExternalInput").ap())
    args.append(nc.dram_tensor("out", inputs["x"].shape, F32, kind="ExternalOutput").ap())
    trunk(nc, *args)
    return run_bass_kernel_spmd(nc, [arrays], core_ids=[0]).results[0]["out"]
```
